# Optimizing a Trainium2 kernel written in Bass

```python
import math
import jax
import jax.numpy as jnp
from jax import lax
import numpy as np

D_MODEL = 1024
BATCH = 1
SEQ = 256
DEPTH = 2

HEAD_DIM = 64
MIX_HALF = D_MODEL // 2
SGU_GROUPS = 4
SGU_WIDTH = MIX_HALF
SGU_GROUP_DIM = SGU_WIDTH // SGU_GROUPS
CHUNK = 128
DIFF_HEADS = MIX_HALF // (2 * HEAD_DIM)
DIFF_QK = DIFF_HEADS * 2 * HEAD_DIM
DIFF_V = DIFF_HEADS * 2 * HEAD_DIM
Q_BLOCK = 128
DIL_PAIRS = ((128, 1), (512, 4), (2048, 16))
DIL_GROUPS = len(DIL_PAIRS)
DIL_HEADS = MIX_HALF // HEAD_DIM
DIL_WIDTH = DIL_HEADS * HEAD_DIM
WIN_BLOCK = 128
CONV_WIDTH = MIX_HALF
CONV_K = 31
EVEN_IN = 2 * SGU_WIDTH + 2 * DIFF_QK + DIFF_V
ODD_IN = 2 * DIL_GROUPS * DIL_WIDTH + DIL_WIDTH + 2 * CONV_WIDTH
MIX_OUT = SGU_WIDTH + DIFF_V
N_EVEN = (DEPTH + 1) // 2
N_ODD = DEPTH // 2
N_EXPERTS = 16
N_EXPERT_GROUPS = 4
EXPERTS_PER_GROUP = N_EXPERTS // N_EXPERT_GROUPS
TOP_K = 2
EXPERT_FF = D_MODEL // 2
RMS_EPS = 1e-6
LN_EPS = 1e-5

kernel_name = 'hybrid_sgu_diffattn_dilated_conformer_moe'

def rms_norm(x, g):
    xf = x.astype(jnp.float32)
    y = xf * lax.rsqrt(jnp.mean(xf * xf, axis=-1, keepdims=True) + RMS_EPS)
    return (y * g.astype(jnp.float32)).astype(x.dtype)

def layer_norm(x, g, b):
    xf = x.astype(jnp.float32)
    mu = jnp.mean(xf, axis=-1, keepdims=True)
    var = jnp.mean(jnp.square(xf - mu), axis=-1, keepdims=True)
    y = (xf - mu) * lax.rsqrt(var + LN_EPS)
    return (y * g.astype(jnp.float32) + b.astype(jnp.float32)).astype(x.dtype)

def alibi_slopes(n_heads):
    return 2.0 ** (-8.0 * jnp.arange(1, n_heads + 1, dtype=jnp.float32) / n_heads)

def split_cols(x, sizes):
    outs, start = [], 0
    for s in sizes:
        outs.append(x[..., start:start + s])
        start += s
    return outs

def spatial_gating(u, v, ln_g, ln_b, w_s, b_s):
    bsz, seq, _ = v.shape
    v = layer_norm(v, ln_g, ln_b).reshape(bsz, seq // CHUNK, CHUNK, SGU_GROUPS, SGU_GROUP_DIM)
    causal = jnp.tril(jnp.ones((CHUNK, CHUNK), dtype=bool))
    w = jnp.where(causal, w_s, jnp.zeros_like(w_s))
    mixed = jnp.einsum('gts,bcsgd->bctgd', w, v) + b_s.T[None, None, :, :, None]
    return u * mixed.reshape(bsz, seq, SGU_WIDTH)

def differential_attention(q, k, v, lam, subln_g, lam_init):
    bsz, n_heads, _, seq, dh = q.shape
    n_blk = seq // Q_BLOCK
    scale = dh ** -0.5
    slopes = alibi_slopes(n_heads)
    k_pos = jnp.arange(seq)
    q_blocks = jnp.moveaxis(q.reshape(bsz, n_heads, 2, n_blk, Q_BLOCK, dh), 3, 0)

    def one_block(args):
        q_blk, blk = args
        q_pos = blk * Q_BLOCK + jnp.arange(Q_BLOCK)
        dist = q_pos[:, None] - k_pos[None, :]
        bias = -slopes[:, None, None] * dist.astype(jnp.float32)
        s = jnp.einsum('bhmqd,bhmkd->bhmqk', q_blk, k, preferred_element_type=jnp.float32)
        s = jnp.where(dist >= 0, s * scale + bias[None, :, None], -jnp.inf)
        p = jax.nn.softmax(s, axis=-1)
        a = p[:, :, 0] - lam * p[:, :, 1]
        return jnp.einsum('bhqk,bhkd->bhqd', a.astype(v.dtype), v)

    out = lax.map(one_block, (q_blocks, jnp.arange(n_blk)))
    out = jnp.moveaxis(out, 0, 2).reshape(bsz, n_heads, seq, 2 * dh)
    out = rms_norm(out, subln_g) * (1.0 - lam_init)
    return out.transpose(0, 2, 1, 3).reshape(bsz, seq, n_heads * 2 * dh)

def dilated_window_attention(q, k, v, slopes, window, dilation):
    bsz, n_heads, seq, dh = q.shape
    steps = window // dilation
    n_sub = seq // dilation
    n_blk = -(-n_sub // WIN_BLOCK)
    pad = n_blk * WIN_BLOCK - n_sub

    def to_sub(t):
        return t.reshape(bsz, n_heads, n_sub, dilation, dh).transpose(0, 1, 3, 2, 4)

    qs = jnp.pad(to_sub(q), ((0, 0), (0, 0), (0, 0), (0, pad), (0, 0)))
    kv_pad = ((0, 0), (0, 0), (0, 0), (WIN_BLOCK, pad), (0, 0))
    ks = jnp.pad(to_sub(k), kv_pad)
    vs = jnp.pad(to_sub(v), kv_pad)
    blk_shape = (bsz, n_heads, dilation, n_blk, WIN_BLOCK, dh)
    q_b = qs.reshape(blk_shape)

    def band(t):
        prev = t[:, :, :, :n_blk * WIN_BLOCK].reshape(blk_shape)
        cur = t[:, :, :, WIN_BLOCK:].reshape(blk_shape)
        return jnp.concatenate([prev, cur], axis=-2)

    k_b, v_b = band(ks), band(vs)
    i = jnp.arange(WIN_BLOCK)[:, None]
    j = jnp.arange(2 * WIN_BLOCK)[None, :]
    dist = i + WIN_BLOCK - j
    key_pos = (jnp.arange(n_blk)[:, None, None] - 1) * WIN_BLOCK + j[None]
    valid = (dist >= 0) & (dist <= steps) & (key_pos >= 0)
    bias = -slopes[:, None, None] * dist.astype(jnp.float32)
    s = jnp.einsum('bhrnqd,bhrnkd->bhrnqk', q_b, k_b, preferred_element_type=jnp.float32) * dh ** -0.5
    s = jnp.where(valid, s + bias[None, :, None, None], -jnp.inf)
    m = jnp.max(s, axis=-1, keepdims=True)
    p = jnp.exp(s - m)
    den = jnp.sum(p, axis=-1)
    o = jnp.einsum('bhrnqk,bhrnkd->bhrnqd', p.astype(v.dtype), v_b, preferred_element_type=jnp.float32)
    o = (o / den[..., None]).astype(v.dtype)
    lse = m[..., 0] + jnp.log(den)
    o = o.reshape(bsz, n_heads, dilation, n_blk * WIN_BLOCK, dh)[:, :, :, :n_sub]
    o = o.transpose(0, 1, 3, 2, 4).reshape(bsz, n_heads, seq, dh)
    lse = lse.reshape(bsz, n_heads, dilation, n_blk * WIN_BLOCK)[..., :n_sub]
    lse = lse.transpose(0, 1, 3, 2).reshape(bsz, n_heads, seq)
    return o, lse

def even_mixer(h, w_in, w_out, ln_g, ln_b, w_s, b_s, lq1, lk1, lq2, lk2, subln_g, lam_init):
    bsz, seq, _ = h.shape
    proj = h @ w_in
    u, v, q, k, vd = split_cols(proj, (SGU_WIDTH, SGU_WIDTH, DIFF_QK, DIFF_QK, DIFF_V))
    a_out = spatial_gating(jax.nn.gelu(u), jax.nn.gelu(v), ln_g, ln_b, w_s, b_s)
    q = q.reshape(bsz, seq, DIFF_HEADS, 2, HEAD_DIM).transpose(0, 2, 3, 1, 4)
    k = k.reshape(bsz, seq, DIFF_HEADS, 2, HEAD_DIM).transpose(0, 2, 3, 1, 4)
    vd = vd.reshape(bsz, seq, DIFF_HEADS, 2 * HEAD_DIM).transpose(0, 2, 1, 3)
    f32 = jnp.float32
    lam = (jnp.exp(jnp.sum(lq1.astype(f32) * lk1.astype(f32)))
           - jnp.exp(jnp.sum(lq2.astype(f32) * lk2.astype(f32))) + lam_init)
    b_out = differential_attention(q, k, vd, lam, subln_g, lam_init)
    return jnp.concatenate([a_out, b_out], axis=-1) @ w_out

def odd_mixer(h, w_in, w_out, conv_w, conv_b, conv_ln_g, conv_ln_b):
    bsz, seq, _ = h.shape
    proj = h @ w_in
    qc, kc, vc, dc = split_cols(proj, (DIL_GROUPS * DIL_WIDTH, DIL_GROUPS * DIL_WIDTH, DIL_WIDTH, 2 * CONV_WIDTH))

    def group_heads(t):
        return t.reshape(bsz, seq, DIL_GROUPS, DIL_HEADS, HEAD_DIM).transpose(2, 0, 3, 1, 4)

    qg, kg = group_heads(qc), group_heads(kc)
    v = vc.reshape(bsz, seq, DIL_HEADS, HEAD_DIM).transpose(0, 2, 1, 3)
    slopes = alibi_slopes(DIL_HEADS)
    outs, lses = [], []
    for g, (window, dilation) in enumerate(DIL_PAIRS):
        o, lse = dilated_window_attention(qg[g], kg[g], v, slopes, window, dilation)
        outs.append(o)
        lses.append(lse)
    wts = jax.nn.softmax(jnp.stack(lses), axis=0)
    c_out = jnp.sum(wts[..., None].astype(v.dtype) * jnp.stack(outs), axis=0)
    c_out = c_out.transpose(0, 2, 1, 3).reshape(bsz, seq, DIL_WIDTH)
    a, gate = split_cols(dc, (CONV_WIDTH, CONV_WIDTH))
    glu = a * jax.nn.sigmoid(gate)
    conv = lax.conv_general_dilated(glu, conv_w[:, None, :], window_strides=(1,),
                                    padding=((CONV_K - 1, 0),),
                                    dimension_numbers=('NWC', 'WIO', 'NWC'),
                                    feature_group_count=CONV_WIDTH) + conv_b
    d_out = jax.nn.silu(layer_norm(conv, conv_ln_g, conv_ln_b))
    return jnp.concatenate([c_out, d_out], axis=-1) @ w_out

def grouped_moe(h, router_w, router_b, w_gu, w_down):
    bsz, seq, dm = h.shape
    t = h.reshape(bsz * seq, dm)
    probs = jax.nn.softmax((t @ router_w).astype(jnp.float32), axis=-1)
    sel = (probs + router_b.astype(jnp.float32)).reshape(-1, N_EXPERT_GROUPS, EXPERTS_PER_GROUP)
    grp_score = jnp.sum(lax.top_k(sel, TOP_K)[0], axis=-1)
    grp = jnp.argmax(grp_score, axis=-1)
    in_grp = jnp.sum(sel * jax.nn.one_hot(grp, N_EXPERT_GROUPS, dtype=jnp.float32)[:, :, None], axis=1)
    _, local = lax.top_k(in_grp, TOP_K)
    experts = grp[:, None] * EXPERTS_PER_GROUP + local
    p_top = jnp.take_along_axis(probs, experts, axis=-1)
    gates = p_top / jnp.sum(p_top, axis=-1, keepdims=True)
    gate_dense = jnp.sum(jax.nn.one_hot(experts, N_EXPERTS, dtype=jnp.float32) * gates[..., None], axis=1)
    gu = jnp.einsum('td,edf->etf', t, w_gu)
    g, u = split_cols(gu, (EXPERT_FF, EXPERT_FF))
    act = jax.nn.silu(g) * u * gate_dense.T[:, :, None].astype(t.dtype)
    y = jnp.einsum('etf,efd->td', act, w_down)
    return y.reshape(bsz, seq, dm)

def setup_inputs(seed: int = 0) -> dict:
    key = jax.random.key(seed)
    ks = jax.random.split(key, 28)

    def nrm(k, shape, s):
        return jax.random.normal(k, shape, jnp.float32) * s

    return {
        'x': nrm(ks[0], (BATCH, SEQ, D_MODEL), 1.0),
        'c': nrm(ks[1], (BATCH, D_MODEL), 1.0),
        'norm1_g': 1.0 + nrm(ks[2], (DEPTH, D_MODEL), 0.02),
        'norm2_g': 1.0 + nrm(ks[3], (DEPTH, D_MODEL), 0.02),
        'ada_w': nrm(ks[4], (DEPTH, D_MODEL, 6 * D_MODEL), 0.5 * D_MODEL ** -0.5),
        'ada_b': nrm(ks[5], (DEPTH, 6 * D_MODEL), 0.02),
        'ev_w_in': nrm(ks[6], (N_EVEN, D_MODEL, EVEN_IN), D_MODEL ** -0.5),
        'ev_w_out': nrm(ks[7], (N_EVEN, MIX_OUT, D_MODEL), MIX_OUT ** -0.5),
        'sgu_ln_g': 1.0 + nrm(ks[8], (N_EVEN, SGU_WIDTH), 0.02),
        'sgu_ln_b': nrm(ks[9], (N_EVEN, SGU_WIDTH), 0.02),
        'sgu_w': nrm(ks[10], (N_EVEN, SGU_GROUPS, CHUNK, CHUNK), 0.5 * CHUNK ** -0.5),
        'sgu_b': 1.0 + nrm(ks[11], (N_EVEN, SGU_GROUPS, CHUNK), 0.02),
        'lam_q1': nrm(ks[12], (N_EVEN, HEAD_DIM), 0.1),
        'lam_k1': nrm(ks[13], (N_EVEN, HEAD_DIM), 0.1),
        'lam_q2': nrm(ks[14], (N_EVEN, HEAD_DIM), 0.1),
        'lam_k2': nrm(ks[15], (N_EVEN, HEAD_DIM), 0.1),
        'diff_subln_g': 1.0 + nrm(ks[16], (N_EVEN, 2 * HEAD_DIM), 0.02),
        'od_w_in': nrm(ks[17], (N_ODD, D_MODEL, ODD_IN), D_MODEL ** -0.5),
        'od_w_out': nrm(ks[18], (N_ODD, MIX_OUT, D_MODEL), MIX_OUT ** -0.5),
        'conv_w': nrm(ks[19], (N_ODD, CONV_K, CONV_WIDTH), CONV_K ** -0.5),
        'conv_b': nrm(ks[20], (N_ODD, CONV_WIDTH), 0.02),
        'conv_ln_g': 1.0 + nrm(ks[21], (N_ODD, CONV_WIDTH), 0.02),
        'conv_ln_b': nrm(ks[22], (N_ODD, CONV_WIDTH), 0.02),
        'router_w': nrm(ks[23], (D_MODEL, N_EXPERTS), D_MODEL ** -0.5),
        'router_b': nrm(ks[24], (N_EXPERTS,), 0.01),
        'moe_w_gu': nrm(ks[25], (DEPTH, N_EXPERTS, D_MODEL, 2 * EXPERT_FF), D_MODEL ** -0.5),
        'moe_w_down': nrm(ks[26], (DEPTH, N_EXPERTS, EXPERT_FF, D_MODEL), EXPERT_FF ** -0.5),
        'final_g': 1.0 + nrm(ks[27], (D_MODEL,), 0.02),
    }

def reference(x, c, norm1_g, norm2_g, ada_w, ada_b, ev_w_in, ev_w_out, sgu_ln_g, sgu_ln_b,
              sgu_w, sgu_b, lam_q1, lam_k1, lam_q2, lam_k2, diff_subln_g, od_w_in, od_w_out,
              conv_w, conv_b, conv_ln_g, conv_ln_b, router_w, router_b, moe_w_gu, moe_w_down,
              final_g):
    bsz = x.shape[0]
    c_act = jax.nn.silu(c)
    for l in range(DEPTH):
        mod = (c_act @ ada_w[l] + ada_b[l]).reshape(bsz, 6, 1, D_MODEL)
        sh1, sc1, g1, sh2, sc2, g2 = (mod[:, i] for i in range(6))
        h = rms_norm(x, norm1_g[l]) * (1.0 + sc1) + sh1
        i = l // 2
        if l % 2 == 0:
            lam_init = 0.8 - 0.6 * math.exp(-0.3 * l)
            y = even_mixer(h, ev_w_in[i], ev_w_out[i], sgu_ln_g[i], sgu_ln_b[i], sgu_w[i], sgu_b[i],
                           lam_q1[i], lam_k1[i], lam_q2[i], lam_k2[i], diff_subln_g[i], lam_init)
        else:
            y = odd_mixer(h, od_w_in[i], od_w_out[i], conv_w[i], conv_b[i], conv_ln_g[i], conv_ln_b[i])
        x = x + g1 * y
        h = rms_norm(x, norm2_g[l]) * (1.0 + sc2) + sh2
        x = x + g2 * grouped_moe(h, router_w, router_b, moe_w_gu[l], moe_w_down[l])
    return rms_norm(x, final_g)


_drawn_inputs = setup_inputs


def setup_inputs(seed=0):
    import zlib

    import numpy as np

    out = dict(_drawn_inputs(seed))
    spreads = {}
    factors = {'norm1_g': 2.772,
     'sgu_ln_g': 28.604,
     'sgu_ln_b': 26.981,
     'sgu_b': 3.974,
     'lam_q2': 28.348,
     'diff_subln_g': 15.342,
     'conv_b': 11.891,
     'conv_ln_g': 38.944,
     'conv_ln_b': 72.084,
     'final_g': 29.616,
     'norm2_g': 3.149}
    for name, (base, spread) in spreads.items():
        noise = np.random.default_rng([zlib.crc32(name.encode()), seed]).standard_normal(out[name].shape)
        drawn = base * np.exp(spread * noise) if base else spread * noise
        out[name] = jnp.asarray(drawn.astype(out[name].dtype))
    for name, factor in factors.items():
        out[name] = (out[name] * factor).astype(out[name].dtype)
    return out
```

```python
from contextlib import ExitStack

import concourse.bass as bass
from concourse import mybir

ALU = mybir.AluOpType
ACT = mybir.ActivationFunctionType
AX = mybir.AxisListType.X
F32 = mybir.dt.float32
I32 = mybir.dt.int32

P = 128
D = 1024
KC = D // P
T = 2
CAP = 128
PANELS = 6
W = 512
BIG = 1e34
RMS_EPS, LN_EPS = 1e-6, 1e-5
LAM_INIT = 0.2
TAPS = 31

C_C, C_NG, C_ADAB, C_CONVB, C_CLG, C_CLB = 0, 8, 40, 136, 140, 144
C_CONVW = 148
C_SGUB = C_CONVW + 4 * TAPS
C_RW = C_SGUB + 4
C_ALL = C_RW + KC * 16
R_LNG, R_LNB, R_SUBG, R_LAM, R_RB = 0, 512, 1024, 1152, 1408
R_ALL = R_RB + 16

EV_ORDER = [("v", 512), ("q", 1024), ("k", 1536), ("vd", 2048), ("u", 0)]
OD_ORDER = [("gate", 4096), ("a", 3584), ("v", 3072), ("q0", 0), ("k0", 1536), ("q1", 512), ("k1", 2048),
            ("q2", 1024), ("k2", 2560)]


def body_items(ada):
    out = [("G", 0), ("U", 0)]
    for n in range(1, 8):
        out += [("G", n), ("U", n), ("D", n - 1)]
        if ada and n <= 6:
            out.append(("A", n - 1))
    return out + [("D", 7)]


PRE = [[("ada", j) for j in range(4)] + [("in", n) for n, _ in EV_ORDER] + [("ada", 4), ("ada", 5), ("out", 0), ("out", 1)]
       + [("ada", j) for j in range(6, 12)],
       [("in", n) for n, _ in OD_ORDER] + [("out", 0), ("out", 1)]]
BODY = [body_items(True), body_items(False)]
PRE_AT = [0, len(PRE[0]) + 2 * len(BODY[0])]
BODY_AT = [PRE_AT[0] + len(PRE[0]), PRE_AT[1] + len(PRE[1])]
assert all(len(b) % PANELS == 0 for b in BODY)


class Place:

    def __init__(self, at, i=None, per=0):
        self.slot = at % PANELS
        rnd = at // PANELS
        self.landed = 16 * (rnd + 1) if i is None else i * (16 * per // PANELS) + 16 * (rnd + 1)
        self.done = rnd + 1 if i is None else i * (per // PANELS) + rnd + 1
        self.before = rnd if i is None else i * (per // PANELS) + rnd


def pre_place(l, item):
    return Place(PRE_AT[l] + PRE[l].index(item))


def body_place(l, item, i):
    return Place(BODY_AT[l] + BODY[l].index(item), i, len(BODY[l]))


class Turn:

    def __init__(self, per):
        self.per, self.n, self.i, self.l, self.at = per, 0, None, 0, 0

    def enter(self, l, i):
        self.l, self.i, self.at = l, i, self.n

    def leave(self):
        assert self.n - self.at == self.per[self.l], (self.n - self.at, self.per, self.l)
        self.n += self.per[self.l]
        self.i = None

    def value(self, k=0):
        return self.n + k if self.i is None else self.i * self.per[self.l] + (self.n + k)

    def tick(self):
        self.n += 1


TURN_PER = [10, 10]
MISC_PER = [16, 10]

NORM_ROOT = [1, 6, 7, 9, 10]

ATT_SEQ = ["S0", "S1", "F", "T0", "S2", "A0", "T1", "S3", "A1", "F", "T2", "S4", "A2", "T3", "S5", "A3", "F",
           "T4", "A4", "T5", "A5", "F"]


def att_fill(l, j):
    nh, nk, t = (4, P, 0) if j < 2 else (2, 2 * P, 1)
    if l == 0:
        h0 = 4 * j if t == 0 else 2 * (j - 2)
        return t, slice(h0, h0 + nh), nh, nk
    h0 = j if t == 0 else 4 * ((j - 2) // 2) + (j - 2) % 2
    return t, slice(h0, h0 + 2 * nh - 1, 2), nh, nk


def heads_of(s):
    return list(range(s.start, s.stop, s.step or 1))


def trunk(nc, x, cols, rows, gate_b, ada_w, ev_w_in, ev_w_out, sgu_w, od_w_in, od_w_out, w_gu, w_down,
          final_g, out):
    ctx = ExitStack()
    with ctx:
        def sb(name, shape, dt=F32):
            return ctx.enter_context(nc.sbuf_tensor(name, shape, dt))

        def sem(name):
            return ctx.enter_context(nc.semaphore(name))

        ring = sb("ring", [P, PANELS, KC * W])
        xs = sb("xs", [P, T, D])
        xh = sb("xh", [P, T, D])
        hT = sb("hT", [P, KC, T * P])
        gb = sb("gb", [P, 4, D])
        col = sb("col", [P, C_ALL])
        ident = sb("ident", [P, P])
        ones = sb("ones", [P, P])
        tri = sb("tri", [P, P])
        slot_no = sb("slot_no", [P, P])
        slot_all = sb("slot_all", [P, P])
        dist = sb("dist", [P, 4, 2 * P])
        idx = sb("idx", [P, 2 * P], I32)
        small = sb("small", [P, 960])
        flag = sb("flag", [P, 2], I32)
        SCR = 13440
        scr = sb("scr", [P, SCR])
        bank = [ctx.enter_context(nc.psum_tensor(f"bank{b}", [P, 512], F32)) for b in range(8)]
        mixT = xh[:, :, :].rearrange("p t (a n) -> p (t a) n", n=2 * P)

        def panel(s):
            return ring[:, s, :].rearrange("p (c n) -> p c n", c=KC)

        def view(off, *dims, base=scr):
            n = 1
            for d in dims:
                n *= d
            v = base[:, off:off + n]
            if len(dims) == 2:
                v = v.rearrange("p (a b) -> p a b", a=dims[0])
            if len(dims) == 3:
                v = v.rearrange("p (a b c) -> p a b c", a=dims[0], b=dims[1])
            return v

        sm = lambda off, *dims: view(off, *dims, base=small)
        cact = sm(0, 8)
        ssq, rms_t, rstd = sm(8, 2), sm(10, 2), sm(12, 2)
        mod = small[:, 16:80].rearrange("p (l s k) -> p l s k", l=2, s=2)
        nslope = sm(80, 2, 8)
        qscale = sm(96, 4)
        lamrow = sm(100, 8)
        lam_t = sm(108, 4)
        mx = sm(112, 2, 8)
        nm_ev = sm(128, 2, 8)
        den_ev = sm(144, 2, 8)
        rden = sm(160, 2, 8)
        nm_od = sm(176, 3, 16)
        den_od = sm(224, 3, 16)
        e_od = sm(272, 3, 16)
        w_od = sm(320, 3, 16)
        nmin = sm(368, 16)
        wsum = sm(384, 16)
        stat = sm(400, 12)
        mv = sm(412, 4)
        ms4 = sm(416, 8)
        lg = sm(424, 2, 16)
        pr = sm(456, 2, 16)
        sel = sm(488, 2, 16)
        s16 = sm(520, 2, 16)
        oh1 = sm(552, 2, 16)
        oh2 = sm(584, 2, 16)
        gates = sm(616, 2, 16)
        no16 = sm(648, 16)
        g4 = [sm(664 + 8 * k, 2, 4) for k in range(6)]
        oh = sm(712, 2, 4)
        rank = sm(720, 2, 4)
        rank2 = sm(728, 2, 4)
        one2 = [sm(736 + 2 * k, 2) for k in range(6)]
        gslot = sm(748, 2, 4)
        cnt = sm(756, 4)
        cmax = sm(760, 1)
        lam_p = sm(762, 2, 64)
        minus_half = sm(892, 1)

        qT = [view(0, 4, 256), view(1024, 4, 256)]
        kT = [view(2048, 4, 256), view(3072, 4, 256)]
        vv = view(4096, 2, 512)
        uu, vg, vn = view(5120, 2, 512), view(6144, 2, 512), view(7168, 2, 512)
        sc = [view(8192, 512), view(8704, 512)]
        pT = [view(9216, 512), view(9728, 512)]
        oo = view(10240, 512)
        row = view(10752, R_ALL)
        qz = [view(0, 4, 256), view(3072, 4, 256)]
        wT, sgw = view(1024, 4, 128), view(3072, 4, 128)
        acc = [view(12288, 512), view(12800, 512)]
        sg = view(5120, 4, 256)
        glu = view(6144, 4, 286)
        conv = view(7296, 4, 256)
        sc_o = [view(8320, 512), view(8832, 512)]
        pT_o = [view(9344, 512), view(9856, 512)]
        og = view(10368, 3, 16, 64)
        pcur = [view(0, 2, 128), view(256, 2, 128)]
        pt = [view(512, 2, 128), view(768, 2, 128)]
        hg = [view(1024, 8, 128), view(2048, 8, 128)]
        sil = [view(3072, 512), view(3584, 512)]
        act_t = [view(4096, 512), view(4608, 512)]
        actT = [view(5120, 4, 128), view(5632, 4, 128)]
        ysb = view(6144, 1024)
        rb_row = sb("rb_row", [P, 16])
        fgrow = hT[:, 0:4, :].rearrange("p c n -> p (c n)")

        panel_in = [sem(f"panel_in{s}") for s in range(PANELS)]
        panel_done = [sem(f"panel_done{s}") for s in range(PANELS)]
        x_in, cols_in, rows_in, gateb_in, rb_in, fg_in, sguw_in = (sem(n) for n in (
            "x_in", "cols_in", "rows_in", "gateb_in", "rb_in", "fg_in", "sguw_in"))
        out_sem = sem("out_stored")
        const_step, consts, dist_i, dist_done, sguw_masked = (sem(n) for n in (
            "const_step", "consts", "dist_i", "dist_done", "sguw_masked"))
        cact_ready = sem("cact_ready")
        ada_step = sem("ada_step")
        dve_step, act_step = sem("dve_step"), sem("act_step")
        x_ready, ssq_ready, pow_done, xh_ready, xT_ready = (sem(n) for n in (
            "x_ready", "ssq_ready", "pow_done", "xh_ready", "xT_ready"))
        hT_dve, hT_act = sem("hT_dve"), sem("hT_act")
        turn_full, turn_free = sem("turn_full"), sem("turn_free")
        misc_full, misc_free = sem("misc_full"), sem("misc_free")
        fill_done = [sem("fill_done0"), sem("fill_done1")]
        fill_act = [sem("fill_act0"), sem("fill_act1")]
        fill_dve = [sem("fill_dve0"), sem("fill_dve1")]
        score_done, score_out, p_ready, a_ready, lam_part = (sem(n) for n in (
            "score_done", "score_out", "p_ready", "a_ready", "lam_part"))
        lam_exp = sem("lam_exp")
        vn_ready, sgu_mixed, aout_ready, bout_ready = (sem(n) for n in (
            "vn_ready", "sgu_mixed", "aout_ready", "bout_ready"))
        sq_ready, conv_ready, xc_ready, xn_ready, dout_ready, ediff_ready, e_ready, cout_ready = (sem(n) for n in (
            "sq_ready", "conv_ready", "xc_ready", "xn_ready", "dout_ready", "ediff_ready", "e_ready", "cout_ready"))
        conv_step = sem("conv_step")
        lg_done, lgm_ready, pr_ready, oh_ready, rank_done, flag_ready = (sem(n) for n in (
            "lg_done", "lgm_ready", "pr_ready", "oh_ready", "rank_done", "flag_ready"))
        p_built, sil_ready, act_ready, y_out, tail_full, tail_free = (sem(n) for n in (
            "p_built", "sil_ready", "act_ready", "y_out", "tail_full", "tail_free"))
        ov_in = [sem(f"over_in{l}") for l in range(2)]
        ov_pe = [sem(f"over_pe{l}") for l in range(2)]
        ov_dve = [sem(f"over_dve{l}") for l in range(2)]
        ov_act = [sem(f"over_act{l}") for l in range(2)]
        final_ready = sem("final_ready")
        pow_asked = sem("pow_asked")
        half_step = sem("half_step")
        qz_zero = sem("qz_zero")

        ada_v = [ada_w[l].rearrange("(c p) (s j m) -> s j p c m", p=P, s=2, m=W) for l in range(2)]
        ev_v = ev_w_in[0].rearrange("(c p) m -> p c m", p=P)
        od_v = od_w_in[0].rearrange("(c p) m -> p c m", p=P)
        out_v = [w[0].rearrange("(c p) m -> p c m", p=P) for w in (ev_w_out, od_w_out)]
        gu_v = [w_gu[l].rearrange("e (c p) (h f) -> h e p c f", p=P, h=2) for l in range(2)]
        dn_v = [w_down[l].rearrange("e (c p) m -> e p c m", p=P) for l in range(2)]

        def down_panel(s):
            return ring[:, s, :].rearrange("p (c m) -> p c m", c=4)

        FILLS = [[("in", n, h) for n, _ in EV_ORDER for h in range(2)] + [("out", j, t) for j in range(2) for t in range(2)],
                 [("in", n, h) for n, _ in OD_ORDER for h in range(2)] + [("out", j, t) for j in range(2) for t in range(2)]]
        DVE_EMPTIES = [{"k", "vd", 0, 1}, {"a", 0, 1}]

        def emptied(l, f):
            mine = FILLS[l][f][1] in DVE_EMPTIES[l]
            n = sum((FILLS[l][g][1] in DVE_EMPTIES[l]) == mine for g in range(f + 1))
            return (fill_dve if mine else fill_act)[l], n

        def wait_fill(eng, l, f):
            kind, name, h = FILLS[l][f]
            if h == 1:
                pl = pre_place(l, (kind, name))
                eng.wait_ge(panel_done[pl.slot], pl.done)
            else:
                eng.wait_ge(fill_done[l], f // 2 + 1)

        def fill_bank(f):
            return bank[f % 4]

        block = ctx.enter_context(nc.Block())

        @block.sync
        def _(sp):
            def load(pl, dst, src, wait):
                if wait:
                    sp.wait_ge(panel_done[pl.slot], pl.before)
                sp.dma_start(dst, src).then_inc(panel_in[pl.slot], 16)

            def load_pre(l):
                offs = dict(EV_ORDER if l == 0 else OD_ORDER)
                for k, (kind, n) in enumerate(PRE[l]):
                    pl = Place(PRE_AT[l] + k)
                    if kind == "ada":
                        src = ada_v[l][n // 6, n % 6]
                    elif kind == "in":
                        src = (ev_v if l == 0 else od_v)[:, :, offs[n]:offs[n] + W]
                    else:
                        src = out_v[l][:, :, n * W:(n + 1) * W]
                    load(pl, panel(pl.slot), src, PRE_AT[l] + k >= PANELS)

            def load_body(l):
                with sp.Fori(0, 2) as i:
                    for k, (kind, n) in enumerate(BODY[l]):
                        pl = Place(BODY_AT[l] + k, i, len(BODY[l]))
                        if kind == "A":
                            load(pl, panel(pl.slot), ada_v[1][i, n], True)
                        elif kind == "D":
                            load(pl, down_panel(pl.slot), dn_v[l][i * 8 + n], True)
                        else:
                            load(pl, panel(pl.slot), gu_v[l][0 if kind == "G" else 1, i * 8 + n], True)

            def overflow(l):
                sp.wait_ge(flag_ready, l + 1)
                over = sp.value_load(flag[0:1, l:l + 1])
                with sp.If(over > 0):
                    end = BODY_AT[l] + 2 * len(BODY[l])
                    for at in range(end - PANELS, end):
                        sp.wait_ge(panel_done[at % PANELS], at // PANELS + 1)
                    with sp.Fori(0, 4) as g:
                        for e in range(4):
                            sp.wait_ge(ov_pe[l], g * 15 + (1 if e == 0 else 2 + 3 * e))
                            sp.dma_start(panel(0), gu_v[l][0, g * 4 + e]).then_inc(ov_in[l], 16)
                            sp.dma_start(panel(1), gu_v[l][1, g * 4 + e]).then_inc(ov_in[l], 16)
                            sp.dma_start(down_panel(2), dn_v[l][g * 4 + e]).then_inc(ov_in[l], 16)
                    sp.wait_ge(ov_pe[l], 60)

            for l in range(2):
                load_pre(l)
                load_body(l)
                overflow(l)

        @block.gpsimd
        def _(pool):
            pool.memset(ones[:, :], 1.0).then_inc(const_step, 1)
            pool.memset(ident[:, :], 0.0).then_inc(const_step, 1)
            pool.wait_ge(const_step, 2)
            pool.affine_select(out=ident[:, :], in_=ident[:, :], compare_op=ALU.not_equal, fill=1.0, base=0,
                               pattern=[[-1, P]], channel_multiplier=1).then_inc(consts, 1)
            pool.affine_select(out=tri[:, :], in_=ones[:, :], compare_op=ALU.is_gt, fill=0.0, base=0,
                               pattern=[[1, P]], channel_multiplier=-1).then_inc(consts, 1)
            pool.iota(slot_all[:, :], [[1, P]], base=0, channel_multiplier=0,
                      allow_small_or_imprecise_dtypes=True).then_inc(const_step, 1)
            pool.wait_ge(const_step, 3)
            pool.affine_select(out=slot_no[:, :], in_=slot_all[:, :], compare_op=ALU.is_gt, fill=-1.0, base=CAP,
                               pattern=[[-1, P]], channel_multiplier=0).then_inc(consts, 1)
            pool.iota(no16, [[1, 16]], base=0, channel_multiplier=0,
                      allow_small_or_imprecise_dtypes=True).then_inc(consts, 1)
            for v in range(8):
                pool.memset(nslope[:, 0, v:v + 1], -(2.0 ** (-2 * (v // 2 + 1))))
                last = pool.memset(nslope[:, 1, v:v + 1], -(2.0 ** -(v + 1)))
            last.then_inc(half_step, 1)
            for c in range(4):
                pool.wait_ge(half_step, 2 * c + 1)
                pool.memset(qscale[:, c:c + 1], 0.125 * 2.0 ** (2 * c + 2)).then_inc(half_step, 1)
                pool.wait_ge(half_step, 2 * c + 2)
                pool.memset(qscale[0:64, c:c + 1], 0.125 * 2.0 ** (2 * c + 1)).then_inc(half_step, 1)
            pool.wait_ge(half_step, 9)
            pool.memset(minus_half, -0.5).then_inc(consts, 1)
            pool.iota(idx[:, :], [[-1, 2 * P]], base=P + 256, channel_multiplier=1).then_inc(dist_i, 1)
            pool.iota(dist[:, 1, :], [[-1, 2 * P]], base=P, channel_multiplier=1,
                      allow_small_or_imprecise_dtypes=True).then_inc(const_step, 1)
            pool.wait_ge(const_step, 4)
            pool.affine_select(out=dist[:, 0, :], in_=dist[:, 1, :], compare_op=ALU.is_ge, fill=BIG, base=P,
                               pattern=[[-1, 2 * P]], channel_multiplier=1).then_inc(const_step, 1)
            pool.wait_ge(const_step, 5)
            pool.affine_select(out=dist[:, 1, :], in_=dist[:, 0, :], compare_op=ALU.is_ge, fill=BIG, base=0,
                               pattern=[[1, 2 * P]], channel_multiplier=-1).then_inc(dist_i, 1)
            pool.wait_ge(sguw_in, 16)
            pool.affine_select(out=sgw, in_=sgw, compare_op=ALU.is_ge, fill=0.0, base=0,
                               pattern=[[0, 4], [-1, P]], channel_multiplier=1).then_inc(sguw_masked, 1)
            pool.wait_ge(panel_done[2], 1)
            pool.dma_start(gb[:, :, :].rearrange("p a n -> p (a n)"),
                           gate_b.partition_broadcast(P)).then_inc(gateb_in, 16)
            roots = [(rstd, rms_t), (mv[:, 2:3], mv[:, 3:4]), (mv[:, 2:3], mv[:, 3:4]),
                     (ms4[:, 4:8], ms4[:, 0:4]), (ms4[:, 4:8], ms4[:, 0:4]), (rstd, rms_t), (rstd, rms_t),
                     (sg[:, 0, :], sg[:, 0, :]), (rstd, rms_t), (rstd, rms_t)]

            def root(n):
                to, of = roots[n]
                pool.wait_ge(pow_asked, n + 1)
                pool.tensor_tensor(to, of, minus_half.to_broadcast([P, of.shape[1]]), ALU.pow).then_inc(pow_done, 1)

            for n in range(9):
                root(n)
            pool.wait_ge(flag_ready, 2)
            pool.dma_start(fgrow, final_g.partition_broadcast(P)).then_inc(fg_in, 16)
            root(9)

        @block.tensor
        def _(pe):
            turn, misc = Turn(TURN_PER), Turn(MISC_PER)

            def take(which):
                sems = turn_free if which is turn else misc_free
                if which.n or which.i is not None:
                    pe.wait_ge(sems, which.value())

            def give(which, ins):
                ins.then_inc(turn_full if which is turn else misc_full, 1)
                which.tick()

            def transposes(blocks, which=None, rows_=P):
                which = which or turn
                b = bank[6] if which is turn else bank[7]
                take(which)
                for k, src in enumerate(blocks):
                    ins = pe.transpose(b[:, k * P:(k + 1) * P], src, ident[:, :])
                give(which, ins)

            def norm_T(ph):
                pe.wait_ge(xh_ready, 2 * (ph + 1))
                for b in range(4):
                    for k in range(4):
                        c, t = 2 * b + k // 2, k % 2
                        ins = pe.transpose(bank[b][:, k * P:(k + 1) * P], xh[:, t, c * P:(c + 1) * P], ident[:, :])
                    ins.then_inc(xT_ready, 1)
                pe.wait_ge(hT_dve, 4 * (ph + 1))
                pe.wait_ge(hT_act, 4 * (ph + 1))

            def ada_sum(a, j, pl):
                take(misc)
                pe.wait_ge(panel_done[pl.slot], pl.done)
                if j % 6 < 4:
                    for m in range(4):
                        ins = pe.matmul(bank[7][:, m:m + 1], acc[a][:, m * P:(m + 1) * P], ones[:, 0:1],
                                        start=True, stop=True)
                else:
                    ins = pe.matmul(bank[7][:, :], ones[:, :], acc[a], start=True, stop=True)
                give(misc, ins)

            def fill(l, f):
                kind, name, h = FILLS[l][f]
                pl = pre_place(l, (kind, name))
                if f >= 4:
                    pe.wait_ge(*emptied(l, f - 4))
                if h == 0:
                    pe.wait_ge(panel_in[pl.slot], pl.landed)
                w, b = panel(pl.slot), fill_bank(f)
                if kind == "out":
                    for c in range(KC):
                        ins = pe.matmul(b[:, :], mixT[:, c, h * P:(h + 1) * P], w[:, c, :],
                                        start=(c == 0), stop=(c == KC - 1))
                elif name in ("v", "u", "vd"):
                    for c in range(KC):
                        ins = pe.matmul(b[:, :], hT[:, c, h * P:(h + 1) * P], w[:, c, :],
                                        start=(c == 0), stop=(c == KC - 1))
                else:
                    for m in range(2):
                        for c in range(KC):
                            ins = pe.matmul(b[:, m * 256:(m + 1) * 256], w[:, c, (2 * h + m) * P:(2 * h + m + 1) * P],
                                            hT[:, c, :], start=(c == 0), stop=(c == KC - 1))
                if h == 1:
                    ins.then_inc(panel_done[pl.slot], 1)
                else:
                    ins.then_inc(fill_done[l], 1)

            def attention(l, g, between):
                base = 6 * (g if l == 0 else g + 1)
                q, k = qT[g % 2], kT[g % 2]
                s_, p_ = (sc, pT) if l == 0 else (sc_o, pT_o)
                todo = list(between)
                for step in ATT_SEQ:
                    if step == "F":
                        if todo:
                            for f in todo.pop(0):
                                f()
                        continue
                    j = int(step[1])
                    n = base + j
                    t, hs, nh, nk = att_fill(l, j)
                    if step[0] == "S":
                        if n >= 2:
                            pe.wait_ge(score_out, n - 1)
                        for v, h in enumerate(heads_of(hs)):
                            if l == 0:
                                q, r = qz[h % 2], slice(0, P)
                            else:
                                r = slice(64 * (h % 2), 64 * (h % 2) + 64)
                            ins = pe.matmul(bank[4 + n % 2][:, v * nk:(v + 1) * nk],
                                            q[r, h // 2, t * P:(t + 1) * P], k[r, h // 2, 0:nk],
                                            start=True, stop=True)
                        ins.then_inc(score_done, 1)
                    elif step[0] == "T":
                        pe.wait_ge(*((a_ready, n + 1) if l == 0 else (p_ready, n + 1)))
                        if l == 0:
                            blocks = [s_[n % 2][:, o:o + P] for o in ((0, 2 * P) if t == 0 else (0, P))]
                        else:
                            blocks = [s_[n % 2][:, o * P:(o + 1) * P] for o in range(4)]
                        transposes(blocks)
                    else:
                        if j in (0, 2):
                            take(misc)
                        pe.wait_ge(turn_free, at_turn[n])
                        nb = t + 1
                        heads = [h // 2 for h in heads_of(hs)][::2] if l == 0 else heads_of(hs)
                        wd = P if l == 0 else 64
                        for v, h in enumerate(heads):
                            for kb in range(nb):
                                ins = pe.matmul(bank[7][:, h * wd:(h + 1) * wd],
                                                p_[n % 2][:, (v * nb + kb) * P:(v * nb + kb + 1) * P],
                                                vv[:, kb, h * wd:(h + 1) * wd],
                                                start=(kb == 0), stop=(kb == nb - 1))
                        if j in (1, 5):
                            give(misc, ins)
                    if step[0] == "T":
                        at_turn[n] = turn.n

            at_turn = {}

            def even():
                base = 0
                for f in range(2 * 3):
                    fill(0, f)
                pe.wait_ge(*emptied(0, 3))
                pe.wait_ge(qz_zero, 1)
                pe.wait_ge(*emptied(0, 5))
                attention(0, 0, [[lambda: (fill(0, 6), fill(0, 7), pe.wait_ge(*emptied(0, 7)))],
                                 [lambda: fill(0, 8)], [lambda: fill(0, 9)]])
                pe.wait_ge(score_out, 6)
                pe.wait_ge(vn_ready, 2)
                for t in range(T):
                    for g in range(4):
                        ins = pe.matmul(bank[4 + t][:, g * P:(g + 1) * P], wT[:, g, :], vn[:, t, g * P:(g + 1) * P],
                                        start=True, stop=True)
                    ins.then_inc(sgu_mixed, 1)
                for t in range(T):
                    pe.wait_ge(aout_ready, t + 1)
                    transposes([uu[:, t, c * P:(c + 1) * P] for c in range(4)])
                for t in range(T):
                    pe.wait_ge(bout_ready, t + 1)
                    transposes([vg[:, t, c * P:(c + 1) * P] for c in range(4)])
                for j in (4, 5):
                    ada_sum(j % 2, j, pre_place(0, ("ada", j)))
                pe.wait_ge(turn_free, turn.n)
                for f in range(10, 14):
                    fill(0, f)
                for j in range(6, 12):
                    ada_sum(j % 2, j, pre_place(0, ("ada", j)))

            def odd():
                for f in range(10):
                    fill(1, f)
                pe.wait_ge(*emptied(1, 9))
                F = lambda f: (lambda: fill(1, f))

                def conv_sum(src, ready, n):
                    def f():
                        take(misc)
                        pe.wait_ge(ready, n)
                        for c in range(4):
                            ins = pe.matmul(bank[7][:, 0:256], ones[:, :], src[:, c, :], start=(c == 0), stop=(c == 3))
                        give(misc, ins)
                    return f

                attention(1, 0, [[F(10)], [F(11)], [F(12)], [F(13)]])
                conv_sum(conv, conv_ready, 1)()
                pe.wait_ge(*emptied(1, 13))
                attention(1, 1, [[F(14), conv_sum(sg, sq_ready, 1)], [F(15)], [F(16)], [F(17)]])
                pe.wait_ge(*emptied(1, 17))
                attention(1, 2, [])
                for t in range(T):
                    pe.wait_ge(cout_ready, 1)
                    transposes([qT[0].rearrange("p a b -> p (a b)")[:, t * 512 + c * P:t * 512 + (c + 1) * P]
                                for c in range(4)])
                pe.wait_ge(turn_free, turn.n)
                pe.wait_ge(dout_ready, 4)
                for f in range(18, 22):
                    fill(1, f)

            def route(l):
                take(misc)
                for t in range(T):
                    for c in range(KC):
                        ins = pe.matmul(bank[7][:, t * 16:(t + 1) * 16], hT[:, c, t * P:(t + 1) * P],
                                        col[:, C_RW + c * 16:C_RW + (c + 1) * 16], start=(c == 0), stop=(c == KC - 1))
                give(misc, ins)
                take(misc)
                pe.wait_ge(oh_ready, l + 1)
                pe.matmul(bank[7][:, 0:4], tri[:, :], oh[:, 0, :], start=True, stop=True)
                pe.matmul(bank[7][:, 4:8], ones[:, :], oh[:, 0, :], start=True, stop=False)
                pe.matmul(bank[7][:, 4:8], tri[:, :], oh[:, 1, :], start=False, stop=True)
                pe.matmul(bank[7][:, 8:12], ones[:, :], oh[:, 0, :], start=True, stop=False)
                ins = pe.matmul(bank[7][:, 8:12], ones[:, :], oh[:, 1, :], start=False, stop=True)
                give(misc, ins)

            def slot_gates(gg, g):
                take(misc)
                for t in range(T):
                    ins = pe.matmul(bank[7][:, 0:4], pcur[gg][:, t, :], gates[:, t, bass.ds(g * 4, 4)],
                                    start=(t == 0), stop=(t == T - 1))
                give(misc, ins)

            def gather(gg, half):
                which, b = ((turn, bank[6]), (misc, bank[7]))[half]
                take(which)
                for c in range(4):
                    cc = 4 * half + c
                    for t in range(T):
                        ins = pe.matmul(b[:, c * P:(c + 1) * P], xh[:, t, cc * P:(cc + 1) * P], pcur[gg][:, t, :],
                                        start=(t == 0), stop=(t == T - 1))
                give(which, ins)

            def scatter(gg, k, b):
                t, h = k // 2, k % 2
                return pe.matmul(b[:, :], pt[gg][:, t, :], ysb[:, h * W:(h + 1) * W], start=True, stop=True)

            def experts(l):
                with pe.Fori(0, 2) as i:
                    turn.enter(l, i)
                    misc.enter(l, i)
                    n0 = 16 * l
                    pe.wait_ge(p_built, i * 2 + (4 * l + 1))
                    slot_gates(0, i * 2)
                    gather(0, 0)
                    gather(0, 1)
                    act_at = {}

                    def up(n, kind):
                        b = bank[2 * (n % 2) + (kind == "U")]
                        pl = body_place(l, (kind, n), i)
                        pe.wait_ge(panel_in[pl.slot], pl.landed)
                        if n >= 2:
                            pe.wait_ge(sil_ready if kind == "G" else act_ready, i * 8 + (n0 + n - 1))
                        h = hg[n // 4]
                        for c in range(KC):
                            ins = pe.matmul(b[:, :], h[:, c, :], panel(pl.slot)[:, c, :], start=(c == 0), stop=(c == KC - 1))
                        ins.then_inc(panel_done[pl.slot], 1)

                    def act_T(n):
                        pe.wait_ge(act_ready, i * 8 + (n0 + n + 1))
                        transposes([act_t[n % 2][:, c * P:(c + 1) * P] for c in range(4)])
                        act_at[n] = turn.value()

                    def down(n):
                        pl = body_place(l, ("D", n), i)
                        pe.wait_ge(panel_in[pl.slot], pl.landed)
                        pe.wait_ge(turn_free, act_at[n])
                        if n == 4:
                            pe.wait_ge(y_out, i * 2 + (4 * l + 1))
                        w = down_panel(pl.slot)
                        for c in range(4):
                            for h in range(2):
                                ins = pe.matmul(bank[4 + h][:, :], actT[n % 2][:, c, :], w[:, c, h * W:(h + 1) * W],
                                                start=(n % 4 == 0 and c == 0), stop=(n % 4 == 3 and c == 3),
                                                skip_group_check=True)
                        ins.then_inc(panel_done[pl.slot], 1)

                    def misc_scatter(k):
                        take(misc)
                        pe.wait_ge(y_out, i * 2 + (4 * l + 1))
                        give(misc, scatter(0, k, bank[7]))

                    for n in range(8):
                        if n in (0, 4):
                            pe.wait_ge(turn_free, hg_turn(turn, n))
                            pe.wait_ge(misc_free, hg_misc(misc, n))
                        up(n, "G")
                        if n >= 1:
                            act_T(n - 1)
                        if n == 0:
                            transposes([pcur[0][:, t, :] for t in range(T)], misc)
                        if n == 2:
                            pe.wait_ge(p_built, i * 2 + (4 * l + 2))
                            slot_gates(1, i * 2 + 1)
                            gather(1, 0)
                        if n in (5, 6):
                            misc_scatter(0 if n == 5 else 3)
                        up(n, "U")
                        if n == 2:
                            gather(1, 1)
                            save["t"], save["m"] = turn.value(), misc.value()
                        if n == 3:
                            transposes([pcur[1][:, t, :] for t in range(T)], misc)
                        if n == 5:
                            misc_scatter(1)
                        if n >= 1:
                            down(n - 1)
                        if l == 0 and 1 <= n <= 6:
                            ada_sum((n - 1) % 2, n - 1, body_place(0, ("A", n - 1), i))
                        if n == 5:
                            misc_scatter(2)
                    act_T(7)
                    down(7)
                    pe.wait_ge(y_out, i * 2 + (4 * l + 2))
                    for k in range(4):
                        scatter(1, k, bank[k]).then_inc(tail_full, 1)
                    turn.leave()
                    misc.leave()

            save = {}

            def hg_turn(turn_, n):
                return turn_.value() if n == 0 else save["t"]

            def hg_misc(misc_, n):
                return misc_.value() if n == 0 else save["m"]

            def overflow(l):
                pe.wait_ge(flag_ready, l + 1)
                over = pe.value_load(flag[0:1, l:l + 1])
                with pe.If(over > 0):
                    pe.wait_ge(tail_free, 8 * (l + 1))
                    with pe.Fori(0, 4) as g:
                        d, q = g * 13, g * 4
                        pe.wait_ge(ov_dve[l], d + 1)
                        for t in range(T):
                            pe.transpose(bank[7][:, t * P:(t + 1) * P], pcur[0][:, t, :], ident[:, :])
                        for t in range(T):
                            ins = pe.matmul(bank[7][:, 256:260], pcur[0][:, t, :], gates[:, t, bass.ds(g * 4, 4)],
                                            start=(t == 0), stop=(t == T - 1))
                        ins.then_inc(ov_pe[l], 1)
                        pe.wait_ge(ov_dve[l], d + 2)
                        for cc in range(KC):
                            for t in range(T):
                                ins = pe.matmul(bank[6 + cc // 4][:, (cc % 4) * P:(cc % 4 + 1) * P],
                                                xh[:, t, cc * P:(cc + 1) * P], pcur[0][:, t, :],
                                                start=(t == 0), stop=(t == T - 1))
                        ins.then_inc(ov_pe[l], 1)
                        pe.wait_ge(ov_dve[l], d + 3)
                        for e in range(4):
                            pe.wait_ge(ov_in[l], g * 192 + 48 * (e + 1))
                            for k in range(2):
                                for c in range(KC):
                                    ins = pe.matmul(bank[k][:, :], hg[0][:, c, :], panel(k)[:, c, :],
                                                    start=(c == 0), stop=(c == KC - 1))
                            ins.then_inc(ov_pe[l], 1)
                            pe.wait_ge(ov_dve[l], d + (4 + 2 * e))
                            for c in range(4):
                                ins = pe.transpose(bank[6][:, c * P:(c + 1) * P], act_t[0][:, c * P:(c + 1) * P], ident[:, :])
                            ins.then_inc(ov_pe[l], 1)
                            pe.wait_ge(ov_dve[l], d + (5 + 2 * e))
                            for c in range(4):
                                for h in range(2):
                                    ins = pe.matmul(bank[4 + h][:, :], actT[0][:, c, :],
                                                    down_panel(2)[:, c, h * W:(h + 1) * W],
                                                    start=(e == 0 and c == 0), stop=(e == 3 and c == 3),
                                                    skip_group_check=True)
                            ins.then_inc(ov_pe[l], 1)
                        pe.wait_ge(ov_dve[l], d + 12)
                        for k in range(4):
                            ins = scatter(0, k, bank[k])
                        ins.then_inc(ov_pe[l], 1)
                        pe.wait_ge(ov_dve[l], d + 13)
                    pe.wait_ge(ov_dve[l], 52)

            pe.wait_ge(consts, 2)
            pe.wait_ge(sguw_masked, 1)
            transposes([sgw[:, g, :] for g in range(4)])
            for j in range(4):
                ada_sum(j % 2, j, pre_place(0, ("ada", j)))
            norm_T(0)
            even()
            norm_T(1)
            route(0)
            experts(0)
            overflow(0)
            norm_T(2)
            odd()
            norm_T(3)
            route(1)
            experts(1)
            overflow(1)

        @block.scalar
        def _(act):
            turn = Turn(TURN_PER)
            steps = [0]

            def turn_copy(dst, n):
                act.wait_ge(turn_full, turn.value(1))
                turn.tick()
                act.activation(dst, n, ACT.Copy).then_inc(turn_free, 1)

            def norm(ph):
                if ph == 0:
                    act.wait_ge(x_in, 16)
                else:
                    act.wait_ge(x_ready, ph + 1)
                for t in range(T):
                    act.activation(xh[:, t, :], xs[:, t, :], ACT.Square, accum_out=ssq[:, t:t + 1])\
                       .then_inc(ssq_ready, 1)
                if ph == 4:
                    return
                act.wait_ge(pow_done, NORM_ROOT[ph])
                for t in range(T):
                    act.activation(xh[:, t, :], xs[:, t, :], ACT.Copy, scale=rstd[:, t:t + 1]).then_inc(xh_ready, 1)
                l, s = ph // 2, ph % 2
                if ph == 0:
                    act.wait_ge(x_ready, 1)
                for c in range(4, 8):
                    act.wait_ge(xT_ready, 4 * ph + c // 2 + 1)
                    act.activation(hT[:, c, :], bank[c // 2][:, 256 * (c % 2):256 * (c % 2) + 256], ACT.Identity,
                                   scale=mod[:, l, s, 8 + c:9 + c], bias=mod[:, l, s, c:c + 1]).then_inc(hT_act, 1)

            def exps(l, n, j, s_, nm, den):
                t, hs, nh, nk = att_fill(l, j)
                act.wait_ge(score_out, n + 1)
                for v, h in enumerate(heads_of(hs)):
                    slope = 2.0 ** (-2 * (h // 2 + 1)) if l == 0 else 2.0 ** -(h + 1)
                    o = s_[n % 2][:, v * nk:(v + 1) * nk]
                    ins = act.activation(o, o, ACT.Exp, scale=slope, bias=nm[:, h:h + 1], accum_out=den[:, h:h + 1])
                ins.then_inc(p_ready, 1)

            def attention(l, g, between):
                base = 6 * (g if l == 0 else g + 1)
                s_, p_ = (sc, pT) if l == 0 else (sc_o, pT_o)
                todo = list(between)
                for step in ATT_SEQ:
                    j = int(step[1]) if len(step) > 1 else 0
                    n, t = base + j, att_fill(l, j)[0]
                    if step == "F" and todo:
                        f = todo.pop(0)
                        empty_odd(f)
                    elif step[0] == "S":
                        if l == 0:
                            exps(l, n, j, s_, nm_ev[:, t, :], den_ev[:, t, :])
                        else:
                            exps(l, n, j, s_, nm_od[:, g, 8 * t:8 * t + 8], den_od[:, g, 8 * t:8 * t + 8])
                    elif step[0] == "T":
                        w = 2 * P if l == 0 else 4 * P
                        turn_copy(p_[n % 2][:, 0:w], bank[6][:, 0:w])

            def even():
                for h in range(2):
                    wait_fill(act, 0, h)
                    act.activation(vg[:, h, :], fill_bank(h)[:, :], ACT.Gelu_apprx_tanh).then_inc(fill_act[0], 1)
                for h in range(2):
                    wait_fill(act, 0, 2 + h)
                    for m in range(2):
                        c = 2 * h + m
                        for k in range(2):
                            r = slice(64 * k, 64 * k + 64)
                            ins = act.activation(qz[k][r, c, :], fill_bank(2 + h)[r, m * 256:(m + 1) * 256], ACT.Copy,
                                                 scale=0.125 * 4.0 ** (c + 1))
                    ins.then_inc(fill_act[0], 1)
                act.wait_ge(lam_part, 1)
                act.activation(lam_t[:, 2:4], lam_t[:, 0:2], ACT.Exp).then_inc(lam_exp, 1)
                attention(0, 0, [])
                for h in range(2):
                    wait_fill(act, 0, 8 + h)
                    act.activation(uu[:, h, :], fill_bank(8 + h)[:, :], ACT.Gelu_apprx_tanh).then_inc(fill_act[0], 1)
                for k in range(4):
                    t = k % 2
                    turn_copy(mixT[:, 4 * (k // 2):4 * (k // 2) + 4, t * P:(t + 1) * P],
                              bank[6][:, :].rearrange("p (c n) -> p c n", c=4))

            def empty_odd(f):
                _, name, h = FILLS[1][f]
                wait_fill(act, 1, f)
                b = fill_bank(f)
                if name == "gate":
                    ins = act.activation(sg[:, 2 * h:2 * h + 2, :], b[:, :].rearrange("p (c n) -> p c n", c=2), ACT.Sigmoid)
                elif name == "v":
                    ins = act.activation(vv[:, h, :], b[:, :], ACT.Copy)
                elif name[0] == "q":
                    for m in range(2):
                        c = 2 * h + m
                        ins = act.activation(qT[int(name[1]) % 2][:, c, :], b[:, m * 256:(m + 1) * 256], ACT.Copy,
                                             scale=qscale[:, c:c + 1])
                else:
                    ins = act.activation(kT[int(name[1]) % 2][:, 2 * h:2 * h + 2, :],
                                         b[:, :].rearrange("p (c n) -> p c n", c=2), ACT.Copy)
                ins.then_inc(fill_act[1], 1)

            def odd():
                for f in (0, 1, 4, 5, 6, 7, 8, 9):
                    empty_odd(f)
                attention(1, 0, [10, 11, 12, 13])
                act.wait_ge(xc_ready, 1)
                act.activation(sg, conv, ACT.Square).then_inc(sq_ready, 1)
                attention(1, 1, [14, 15, 16, 17])
                attention(1, 2, [])
                act.wait_ge(ediff_ready, 1)
                act.activation(e_od, e_od, ACT.Exp).then_inc(e_ready, 1)
                act.wait_ge(xn_ready, 1)
                for c in range(4):
                    act.activation(mixT[:, 4 + c, :], conv[:, c, :], ACT.Silu, scale=col[:, C_CLG + c:C_CLG + c + 1],
                                   bias=col[:, C_CLB + c:C_CLB + c + 1]).then_inc(dout_ready, 1)
                for t in range(T):
                    turn_copy(mixT[:, 0:4, t * P:(t + 1) * P], bank[6][:, :].rearrange("p (c n) -> p c n", c=4))

            def route(l):
                act.wait_ge(lgm_ready, l + 1)
                act.activation(pr, lg, ACT.Exp).then_inc(pr_ready, 1)

            def gather_cols(gg, l, half, b, src):
                for c in range(4):
                    cc = 4 * half + c
                    ins = act.activation(hg[gg][:, cc, :], src[:, c * P:(c + 1) * P], ACT.Identity,
                                         scale=mod[:, l, 1, 8 + cc:9 + cc], bias=mod[:, l, 1, cc:cc + 1])
                return ins

            def experts(l):
                with act.Fori(0, 2) as i:
                    turn.enter(l, i)
                    n0 = 16 * l

                    def gather(gg):
                        act.wait_ge(turn_full, turn.value(1))
                        turn.tick()
                        gather_cols(gg, l, 0, None, bank[6]).then_inc(turn_free, 1)

                    def act_T(n):
                        turn_copy(actT[n % 2], bank[6][:, :].rearrange("p (c n) -> p c n", c=4))

                    gather(0)
                    for n in range(8):
                        pl = body_place(l, ("G", n), i)
                        act.wait_ge(panel_done[pl.slot], pl.done)
                        if n >= 2:
                            act.wait_ge(act_ready, i * 8 + (n0 + n - 1))
                        act.activation(sil[n % 2], bank[2 * (n % 2)][:, :], ACT.Silu).then_inc(sil_ready, 1)
                        if n >= 1:
                            act_T(n - 1)
                        if n == 2:
                            gather(1)
                    act_T(7)
                    turn.leave()

            def overflow(l):
                act.wait_ge(flag_ready, l + 1)
                over = act.value_load(flag[0:1, l:l + 1])
                with act.If(over > 0):
                    with act.Fori(0, 4) as g:
                        for e in range(4):
                            act.wait_ge(ov_pe[l], g * 15 + (3 + 3 * e))
                            act.activation(sil[0], bank[0][:, :], ACT.Silu).then_inc(ov_act[l], 1)
                    act.wait_ge(ov_dve[l], 52)

            act.dma_start(xs[:, :, :], x.rearrange("(t p) d -> p t d", p=P)).then_inc(x_in, 16)
            act.dma_start(col[:, :], cols).then_inc(cols_in, 16)
            act.dma_start(sgw, sgu_w[0].rearrange("g t s -> t g s")).then_inc(sguw_in, 16)
            act.dma_start(row, rows[0:1, :].rearrange("a n -> (a n)").partition_broadcast(P)).then_inc(rows_in, 16)
            act.dma_start(rb_row[:, :], rows[0:1, R_RB:R_RB + 16].rearrange("a n -> (a n)").partition_broadcast(P))\
               .then_inc(rb_in, 16)
            act.wait_ge(cols_in, 16)
            act.activation(cact, col[:, C_C:C_C + 8], ACT.Silu).then_inc(cact_ready, 1)
            turn_copy(wT, bank[6][:, :].rearrange("p (c n) -> p c n", c=4))
            for l in range(2):
                norm(2 * l)
                even() if l == 0 else odd()
                norm(2 * l + 1)
                route(l)
                experts(l)
                overflow(l)
            norm(4)
            act.wait_ge(final_ready, 2)
            act.dma_start(out.rearrange("(t p) d -> p t d", p=P), xh[:, :, :]).then_inc(out_sem, 16)
            act.wait_ge(out_sem, 16)

        @block.vector
        def _(dve):
            misc = Turn(MISC_PER)
            steps, turns_seen = [0], {}

            def step(ins):
                steps[0] += 1
                ins.then_inc(dve_step, 1)
                dve.wait_ge(dve_step, steps[0])

            def misc_in():
                dve.wait_ge(misc_full, misc.value(1))
                misc.tick()

            ada_n = [0]

            def ada_acc(j, pl, i=None):
                a = acc[j % 2]
                dve.wait_ge(panel_in[pl.slot], pl.landed)
                w = panel(pl.slot)
                base = 7 * ada_n[0]
                ada_n[0] += 1
                dve.tensor_scalar(a, w[:, 0, :], cact[:, 0:1], None, ALU.mult).then_inc(ada_step, 1)
                for c in range(1, KC):
                    v = base + c
                    dve.wait_ge(ada_step, v if i is None else i * 42 + v)
                    ins = dve.scalar_tensor_tensor(out=a, in0=w[:, c, :], scalar=cact[:, c:c + 1], in1=a,
                                                   op0=ALU.mult, op1=ALU.add)
                    ins.then_inc(*((ada_step, 1) if c < KC - 1 else (panel_done[pl.slot], 1)))

            def ada_out(l, s, j):
                misc_in()
                if j < 4:
                    o = 8 * (j // 2) + 4 * (j % 2)
                    bias = col[:, C_ADAB:C_ADAB + 96].rearrange("p (l s k) -> p l s k", l=2, s=2)
                    dve.tensor_tensor(mod[:, l, s, o:o + 4], bank[7][:, 0:4], bias[:, l, s, o:o + 4], ALU.add)\
                       .then_inc(misc_free, 1)
                else:
                    o = (j - 4) * W
                    g = gb[:, s + 2 * l, o:o + W]
                    dve.tensor_tensor(g, bank[7][:, :], g, ALU.add).then_inc(misc_free, 1)

            def ada_static(js):
                prev = None
                for j in js:
                    ada_acc(j, pre_place(0, ("ada", j)))
                    if prev is not None:
                        ada_out(0, prev // 6, prev % 6)
                    prev = j
                ada_out(0, prev // 6, prev % 6)

            def open_phase(ph):
                l, s = ph // 2, ph % 2
                o = C_NG + 8 * (2 * l + s)
                dve.wait_ge(misc_free, misc.n)
                dve.scalar_tensor_tensor(out=mod[:, l, s, 8:16], in0=mod[:, l, s, 8:16], scalar=1.0,
                                         in1=col[:, o:o + 8], op0=ALU.add, op1=ALU.mult).then_inc(x_ready, 1)

            def rstd_of(ph):
                dve.wait_ge(ssq_ready, 2 * (ph + 1))
                dve.tensor_scalar(rms_t, ssq, 1.0 / D, RMS_EPS, ALU.mult, ALU.add).then_inc(pow_asked, 1)

            def norm(ph):
                rstd_of(ph)
                l, s = ph // 2, ph % 2
                dve.wait_ge(x_ready, ph + 1)
                for c in range(4):
                    dve.wait_ge(xT_ready, 4 * ph + c // 2 + 1)
                    dve.tensor_scalar(hT[:, c, :], bank[c // 2][:, 256 * (c % 2):256 * (c % 2) + 256],
                                      mod[:, l, s, 8 + c:9 + c], mod[:, l, s, c:c + 1],
                                      ALU.mult, ALU.add).then_inc(hT_dve, 1)

            def scores(l, n, j, s_, nm, d):
                t, hs, nh, nk = att_fill(l, j)
                dve.wait_ge(score_done, n + 1)
                if n >= 2 and (l == 0 or n >= 8):
                    dve.wait_ge(turn_full, at_turn_of(l, n - 2))
                o = s_[n % 2].rearrange("p (h k) -> p h k", h=nh)
                step(dve.tensor_tensor(o, bank[4 + n % 2][:, :].rearrange("p (h k) -> p h k", h=nh),
                                       dist[:, d:d + 1, 2 * P - nk:2 * P].to_broadcast([P, nh, nk]), ALU.subtract))
                m = mx[:, t, hs]
                step(dve.tensor_reduce(m, o, AX, ALU.max))
                dve.tensor_tensor(nm[:, hs], m, nslope[:, l, hs], ALU.mult).then_inc(score_out, 1)

            def at_turn_of(l, n):
                if l == 0:
                    return 1 + n + 1
                return 1 + 6 + 4 + 20 + (n - 6) + 1

            def combine(n, j):
                t, hs, nh, nk = att_fill(0, j)
                dve.wait_ge(p_ready, n + 1)
                r = rden[:, t, hs]
                step(dve.reciprocal(r, den_ev[:, t, hs]))
                step(dve.tensor_tensor(r, r, lamrow[:, hs], ALU.mult))
                for v in range(nh // 2):
                    p1 = sc[n % 2][:, 2 * v * nk:(2 * v + 1) * nk]
                    p2 = sc[n % 2][:, (2 * v + 1) * nk:(2 * v + 2) * nk]
                    step(dve.tensor_scalar(p2, p2, r[:, 2 * v + 1:2 * v + 2], None, ALU.mult))
                    ins = dve.scalar_tensor_tensor(out=p1, in0=p1, scalar=r[:, 2 * v:2 * v + 1], in1=p2,
                                                   op0=ALU.mult, op1=ALU.add)
                ins.then_inc(a_ready, 1)

            def sub_norm(t):
                misc_in()
                dve.tensor_copy(oo, bank[7][:, :]).then_inc(misc_free, 1)
                dve.wait_ge(misc_free, misc.n)
                o4 = oo.rearrange("p (h n) -> p h n", h=4)
                b4 = vg[:, t, :].rearrange("p (h n) -> p h n", h=4)
                step(dve.tensor_tensor(vg[:, t, :], oo, oo, ALU.mult))
                step(dve.tensor_reduce(ms4[:, 0:4], b4, AX, ALU.add))
                dve.tensor_scalar(ms4[:, 0:4], ms4[:, 0:4], 1.0 / P, RMS_EPS, ALU.mult, ALU.add).then_inc(pow_asked, 1)
                dve.wait_ge(pow_done, 4 + t)
                step(dve.tensor_tensor(o4, o4, ms4[:, 4:8].unsqueeze(2).to_broadcast([P, 4, P]), ALU.mult))
                dve.scalar_tensor_tensor(out=b4, in0=o4, scalar=1.0 - LAM_INIT,
                                         in1=row[:, R_SUBG:R_SUBG + P].unsqueeze(1).to_broadcast([P, 4, P]),
                                         op0=ALU.mult, op1=ALU.mult).then_inc(bout_ready, 1)

            def residual(l, f):
                for k in range(4):
                    j, t = k // 2, k % 2
                    wait_fill(dve, l, f + k)
                    tmp = scr[:, 8192 + 512 * (k % 2):8704 + 512 * (k % 2)]
                    sem_, n = emptied(l, f + k)
                    dve.tensor_tensor(tmp, fill_bank(f + k)[:, :], gb[:, 2 * l, j * W:(j + 1) * W], ALU.mult)\
                       .then_inc(sem_, 1)
                    dve.wait_ge(sem_, n)
                    xx = xs[:, t, j * W:(j + 1) * W]
                    step(dve.tensor_tensor(xx, xx, tmp, ALU.add))

            def even():
                dve.wait_ge(rows_in, 16)
                for k in range(2):
                    o = R_LAM + 128 * k
                    step(dve.tensor_tensor(lam_p[:, k, :], row[:, o:o + 64], row[:, o + 64:o + 128], ALU.mult))
                dve.tensor_reduce(lam_t[:, 0:2], lam_p, AX, ALU.add).then_inc(lam_part, 1)
                for t in range(T):
                    dve.wait_ge(fill_act[0], t + 1)
                    step(dve.bn_stats(stat[:, 6 * t:6 * t + 6], vg[:, t, :]))
                    step(dve.bn_aggr(mv[:, 0:2], stat[:, 6 * t:6 * t + 6]))
                    dve.tensor_scalar(mv[:, 3:4], mv[:, 1:2], LN_EPS, None, ALU.add).then_inc(pow_asked, 1)
                    dve.wait_ge(pow_done, 2 + t)
                    step(dve.tensor_scalar(vn[:, t, :], vg[:, t, :], mv[:, 0:1], mv[:, 2:3], ALU.subtract, ALU.mult))
                    step(dve.tensor_tensor(vn[:, t, :], vn[:, t, :], row[:, R_LNG:R_LNG + 512], ALU.mult))
                    dve.tensor_tensor(vn[:, t, :], vn[:, t, :], row[:, R_LNB:R_LNB + 512], ALU.add).then_inc(vn_ready, 1)
                dve.wait_ge(lam_exp, 1)
                step(dve.tensor_tensor(lam_t[:, 0:1], lam_t[:, 3:4], lam_t[:, 2:3], ALU.subtract))
                step(dve.memset(lamrow, 1.0))
                lr = lamrow.rearrange("p (h m) -> p h m", m=2)[:, :, 1]
                step(dve.tensor_scalar(lr, lam_t[:, 0:1].to_broadcast([P, 4]), -LAM_INIT, None, ALU.add))
                for h in range(2):
                    wait_fill(dve, 0, 4 + h)
                    dve.tensor_copy(kT[0][:, 2 * h:2 * h + 2, :], fill_bank(4 + h)[:, :].rearrange("p (c n) -> p c n", c=2))\
                       .then_inc(fill_dve[0], 1)
                dve.wait_ge(dist_done, 2)
                scores(0, 0, 0, sc, nm_ev[:, 0, :], 0)
                scores(0, 1, 1, sc, nm_ev[:, 0, :], 0)
                for h in range(2):
                    wait_fill(dve, 0, 6 + h)
                    dve.tensor_copy(vv[:, h, :], fill_bank(6 + h)[:, :]).then_inc(fill_dve[0], 1)
                combine(0, 0)
                for j in range(2, 6):
                    scores(0, j, j, sc, nm_ev[:, 1, :], 0)
                    combine(j - 1, j - 1)
                    if j == 3:
                        sub_norm(0)
                combine(5, 5)
                for t in range(T):
                    dve.wait_ge(sgu_mixed, t + 1)
                    dve.wait_ge(fill_act[0], 5 + t)
                    for g in range(4):
                        o = uu[:, t, g * P:(g + 1) * P]
                        ins = dve.scalar_tensor_tensor(out=o, in0=bank[4 + t][:, g * P:(g + 1) * P],
                                                       scalar=col[:, C_SGUB + g:C_SGUB + g + 1], in1=o,
                                                       op0=ALU.add, op1=ALU.mult)
                    ins.then_inc(aout_ready, 1)
                sub_norm(1)
                dve.wait_ge(gateb_in, 16)
                ada_static([4, 5])
                residual(0, 10)

            def odd():
                step(dve.memset(glu[:, :, 0:TAPS - 1], 0.0))
                for h in range(2):
                    wait_fill(dve, 1, 2 + h)
                    dve.wait_ge(fill_act[1], h + 1)
                    dve.tensor_tensor(glu[:, 2 * h:2 * h + 2, TAPS - 1:TAPS - 1 + 256],
                                      fill_bank(2 + h)[:, :].rearrange("p (c n) -> p c n", c=2),
                                      sg[:, 2 * h:2 * h + 2, :], ALU.mult).then_inc(fill_dve[1], 1)
                dve.wait_ge(fill_dve[1], 2)
                n = 0
                for j in range(TAPS):
                    for c in range(4):
                        src = glu[:, c, j:j + 256]
                        w = col[:, C_CONVW + c * TAPS + j:C_CONVW + c * TAPS + j + 1]
                        if j == 0:
                            ins = dve.tensor_scalar(conv[:, c, :], src, w, col[:, C_CONVB + c:C_CONVB + c + 1],
                                                    ALU.mult, ALU.add)
                        else:
                            dve.wait_ge(conv_step, n - 3)
                            ins = dve.scalar_tensor_tensor(out=conv[:, c, :], in0=src, scalar=w, in1=conv[:, c, :],
                                                           op0=ALU.mult, op1=ALU.add)
                        n += 1
                        if n < 4 * TAPS:
                            ins.then_inc(conv_step, 1)
                        else:
                            ins.then_inc(conv_ready, 1)

                def group(g, extra=None):
                    for j in range(6):
                        t = att_fill(1, j)[0]
                        scores(1, 6 + 6 * g + j, j, sc_o, nm_od[:, g, 8 * t:8 * t + 8], 1 + g)
                        if j == 1 and extra:
                            extra()
                        if j in (3, 5):
                            tt = 0 if j == 3 else 1
                            misc_in()
                            dve.tensor_copy(og[:, g, 8 * tt:8 * tt + 8, :],
                                            bank[7][:, :].rearrange("p (h n) -> p h n", h=8)).then_inc(misc_free, 1)

                group(0)
                misc_in()
                dve.scalar_tensor_tensor(out=conv, in0=bank[7][:, 0:256].unsqueeze(1).to_broadcast([P, 4, 256]),
                                         scalar=-1.0 / 512, in1=conv, op0=ALU.mult, op1=ALU.add).then_inc(misc_free, 1)
                dve.wait_ge(misc_free, misc.n)
                dve.tensor_copy(stat[:, 0:1], conv[:, 0, 0:1]).then_inc(xc_ready, 1)

                def conv_norm():
                    misc_in()
                    var = sg[:, 0, :]
                    dve.tensor_scalar(var, bank[7][:, 0:256], 1.0 / 512, LN_EPS, ALU.mult, ALU.add).then_inc(misc_free, 1)
                    dve.wait_ge(misc_free, misc.n)
                    dve.tensor_copy(stat[:, 1:2], var[:, 0:1]).then_inc(pow_asked, 1)
                    dve.wait_ge(pow_done, 8)
                    dve.tensor_tensor(conv, conv, sg[:, 0:1, :].to_broadcast([P, 4, 256]), ALU.mult).then_inc(xn_ready, 1)

                group(1, conv_norm)
                group(2)
                step(dve.tensor_tensor(nmin, nm_od[:, 0, :], nm_od[:, 1, :], ALU.min))
                step(dve.tensor_tensor(nmin, nmin, nm_od[:, 2, :], ALU.min))
                dve.tensor_tensor(e_od, nmin.unsqueeze(1).to_broadcast([P, 3, 16]), nm_od, ALU.subtract)\
                   .then_inc(ediff_ready, 1)
                dve.wait_ge(e_ready, 1)
                step(dve.tensor_tensor(w_od, e_od, den_od, ALU.mult))
                step(dve.tensor_tensor(wsum, w_od[:, 0, :], w_od[:, 1, :], ALU.add))
                step(dve.tensor_tensor(wsum, wsum, w_od[:, 2, :], ALU.add))
                step(dve.reciprocal(wsum, wsum))
                step(dve.tensor_tensor(w_od, e_od, wsum.unsqueeze(1).to_broadcast([P, 3, 16]), ALU.mult))
                dve.wait_ge(misc_free, misc.n)
                for g in range(3):
                    step(dve.tensor_tensor(og[:, g], og[:, g], w_od[:, g, :].unsqueeze(2).to_broadcast([P, 16, 64]), ALU.mult))
                cc = qT[0].rearrange("p a b -> p (a b)").rearrange("p (h n) -> p h n", h=16)
                step(dve.tensor_tensor(cc, og[:, 0], og[:, 1], ALU.add))
                dve.tensor_tensor(cc, cc, og[:, 2], ALU.add).then_inc(cout_ready, 1)
                residual(1, 18)

            def first_of(dst, vals, width, one, tmp):
                step(dve.tensor_reduce(one, vals, AX, ALU.max))
                bc = one.unsqueeze(2).to_broadcast([P, 2, width])
                no = no16[:, 0:width].unsqueeze(1).to_broadcast([P, 2, width])
                step(dve.tensor_tensor(tmp, vals, bc, ALU.is_lt))
                step(dve.scalar_tensor_tensor(out=tmp, in0=tmp, scalar=64.0, in1=no, op0=ALU.mult, op1=ALU.add))
                step(dve.tensor_reduce(one, tmp, AX, ALU.min))
                step(dve.tensor_tensor(dst, no, bc, ALU.is_equal))

            def route(l):
                misc_in()
                logits = bank[7][:, 0:32].rearrange("p (t e) -> p t e", t=2)
                step(dve.tensor_reduce(one2[0], logits, AX, ALU.max))
                dve.tensor_tensor(lg, logits, one2[0].unsqueeze(2).to_broadcast([P, 2, 16]), ALU.subtract)\
                   .then_inc(misc_free, 1)
                dve.wait_ge(misc_free, misc.n)
                dve.tensor_copy(one2[5][:, 0:1], lg[:, 0, 0:1]).then_inc(lgm_ready, 1)
                dve.wait_ge(pr_ready, l + 1)
                step(dve.tensor_reduce(one2[0], pr, AX, ALU.add))
                step(dve.reciprocal(one2[0], one2[0]))
                step(dve.tensor_tensor(pr, pr, one2[0].unsqueeze(2).to_broadcast([P, 2, 16]), ALU.mult))
                step(dve.tensor_tensor(sel, pr, rb_row[:, :].unsqueeze(1).to_broadcast([P, 2, 16]), ALU.add))
                q = sel.rearrange("p t (g k) -> p t g k", k=4)
                hi1, lo1, hi2, lo2, sc4, tmp4 = g4
                dve.tensor_tensor(hi1, q[:, :, :, 0], q[:, :, :, 1], ALU.max)
                dve.tensor_tensor(lo1, q[:, :, :, 0], q[:, :, :, 1], ALU.min)
                dve.tensor_tensor(hi2, q[:, :, :, 2], q[:, :, :, 3], ALU.max)
                step(dve.tensor_tensor(lo2, q[:, :, :, 2], q[:, :, :, 3], ALU.min))
                step(dve.tensor_tensor(sc4, hi1, hi2, ALU.max))
                step(dve.tensor_tensor(hi1, hi1, hi2, ALU.min))
                step(dve.tensor_tensor(lo1, lo1, lo2, ALU.max))
                step(dve.tensor_tensor(hi1, hi1, lo1, ALU.max))
                step(dve.tensor_tensor(sc4, sc4, hi1, ALU.add))
                first_of(oh, sc4, 4, one2[1], tmp4)
                dve.tensor_copy(one2[5][:, 1:2], oh[:, 0, 0:1]).then_inc(oh_ready, 1)
                for t in range(T):
                    step(dve.tensor_tensor(s16[:, t, :].rearrange("p (g k) -> p g k", k=4), q[:, t],
                                           oh[:, t, :].unsqueeze(2).to_broadcast([P, 4, 4]), ALU.mult))
                    step(dve.tensor_scalar(oh1[:, t, :].rearrange("p (g k) -> p g k", k=4),
                                           oh[:, t, :].unsqueeze(2).to_broadcast([P, 4, 4]), 1e30, -1e30, ALU.mult, ALU.add))
                step(dve.tensor_tensor(s16, s16, oh1, ALU.add))
                first_of(oh1, s16, 16, one2[2], oh2)
                step(dve.scalar_tensor_tensor(out=s16, in0=oh1, scalar=-1e32, in1=s16, op0=ALU.mult, op1=ALU.add))
                first_of(oh2, s16, 16, one2[2], gates)
                step(dve.tensor_tensor(oh1, oh1, oh2, ALU.add))
                step(dve.tensor_tensor(gates, pr, oh1, ALU.mult))
                step(dve.tensor_reduce(one2[3], gates, AX, ALU.add))
                step(dve.reciprocal(one2[3], one2[3]))
                step(dve.tensor_tensor(gates, gates, one2[3].unsqueeze(2).to_broadcast([P, 2, 16]), ALU.mult))
                misc_in()
                step(dve.tensor_copy(rank.rearrange("p t g -> p (t g)"), bank[7][:, 0:8]))
                dve.tensor_copy(cnt, bank[7][:, 8:12]).then_inc(misc_free, 1)
                dve.wait_ge(misc_free, misc.n)
                step(dve.tensor_scalar(rank2, rank, -float(CAP), None, ALU.add))
                step(dve.tensor_reduce(cmax, cnt, AX, ALU.max))
                dve.tensor_scalar(flag[:, l:l + 1], cmax, float(CAP), None, ALU.is_gt).then_inc(flag_ready, 1)

            def slot_map(dst, g, numbers, ranks):
                for t in range(T):
                    ins = dve.tensor_scalar(dst[:, t, :], numbers[:, :], ranks[:, t, bass.ds(g, 1)], oh[:, t, bass.ds(g, 1)],
                                            ALU.is_equal, ALU.mult)
                return ins

            def gather_cols(gg, l, half, src):
                for c in range(4):
                    cc = 4 * half + c
                    ins = dve.tensor_scalar(hg[gg][:, cc, :], src[:, c * P:(c + 1) * P], mod[:, l, 1, 8 + cc:9 + cc],
                                            mod[:, l, 1, cc:cc + 1], ALU.mult, ALU.add)
                return ins

            def y_out_gated(l, s_, n):
                for h in range(2):
                    ins = dve.tensor_tensor(ysb[:, h * W:(h + 1) * W], bank[4 + h][:, :],
                                            gb[:, 2 * l + 1, h * W:(h + 1) * W], ALU.mult)
                ins.then_inc(s_, n)

            def add_x(k, b):
                t, h = k // 2, k % 2
                xx = xs[:, t, h * W:(h + 1) * W]
                return dve.tensor_tensor(xx, b[:, :], xx, ALU.add)

            def experts(l):
                with dve.Fori(0, 2) as i:
                    misc.enter(l, i)
                    n0 = 16 * l
                    ada_n[0] = 12

                    def slot_gates(gg):
                        misc_in()
                        dve.tensor_copy(gslot[:, gg, :], bank[7][:, 0:4]).then_inc(misc_free, 1)

                    def gather(gg):
                        misc_in()
                        gather_cols(gg, l, 1, bank[7]).then_inc(misc_free, 1)

                    def slot_T(gg):
                        misc_in()
                        dve.tensor_copy(pt[gg].rearrange("p t n -> p (t n)"), bank[7][:, 0:256]).then_inc(misc_free, 1)

                    def misc_x(k):
                        misc_in()
                        add_x(k, bank[7]).then_inc(misc_free, 1)

                    def y_group(gg):
                        pl = body_place(l, ("D", 4 * gg + 3), i)
                        dve.wait_ge(panel_done[pl.slot], pl.done)
                        y_out_gated(l, y_out, 1)

                    slot_map(pcur[0], i * 2, slot_no, rank).then_inc(p_built, 1)
                    slot_gates(0)
                    gather(0)
                    for n in range(8):
                        if n == 0:
                            slot_T(0)
                        if n == 2:
                            slot_gates(1)
                        if n in (5, 6):
                            misc_x(0 if n == 5 else 3)
                        pl = body_place(l, ("U", n), i)
                        dve.wait_ge(sil_ready, i * 8 + (n0 + n + 1))
                        dve.wait_ge(panel_done[pl.slot], pl.done)
                        if n in (0, 4):
                            dve.wait_ge(misc_free, misc.value())
                        dve.scalar_tensor_tensor(out=act_t[n % 2], in0=bank[2 * (n % 2) + 1][:, :],
                                                 scalar=gslot[:, n // 4, n % 4:n % 4 + 1], in1=sil[n % 2],
                                                 op0=ALU.mult, op1=ALU.mult).then_inc(act_ready, 1)
                        if n == 1:
                            slot_map(pcur[1], i * 2 + 1, slot_no, rank).then_inc(p_built, 1)
                        if n == 2:
                            gather(1)
                        if n == 3:
                            slot_T(1)
                        if n == 5:
                            misc_x(1)
                        if l == 0 and 1 <= n <= 6:
                            ada_acc(n - 1, body_place(0, ("A", n - 1), i), i)
                        if n == 4:
                            y_group(0)
                        if l == 0 and 1 <= n <= 6:
                            ada_out(1, i, n - 1)
                        if n == 5:
                            misc_x(2)
                    y_group(1)
                    for k in range(4):
                        dve.wait_ge(tail_full, i * 4 + (8 * l + k + 1))
                        add_x(k, bank[k]).then_inc(tail_free, 1)
                    misc.leave()

            def overflow(l):
                dve.wait_ge(flag_ready, l + 1)
                over = dve.value_load(flag[0:1, l:l + 1])
                with dve.If(over > 0):
                    dve.wait_ge(tail_free, 8 * (l + 1))
                    with dve.Fori(0, 4) as g:
                        q, a = g * 15, g * 4
                        slot_map(pcur[0], g, slot_all, rank2).then_inc(ov_dve[l], 1)
                        dve.wait_ge(ov_pe[l], q + 1)
                        dve.tensor_copy(pt[0].rearrange("p t n -> p (t n)"), bank[7][:, 0:256])
                        dve.tensor_copy(gslot[:, 0, :], bank[7][:, 256:260]).then_inc(ov_dve[l], 1)
                        dve.wait_ge(ov_pe[l], q + 2)
                        gather_cols(0, l, 0, bank[6])
                        gather_cols(0, l, 1, bank[7]).then_inc(ov_dve[l], 1)
                        for e in range(4):
                            dve.wait_ge(ov_act[l], a + (e + 1))
                            dve.wait_ge(ov_pe[l], q + (3 + 3 * e))
                            dve.scalar_tensor_tensor(out=act_t[0], in0=bank[1][:, :], scalar=gslot[:, 0, e:e + 1],
                                                     in1=sil[0], op0=ALU.mult, op1=ALU.mult).then_inc(ov_dve[l], 1)
                            dve.wait_ge(ov_pe[l], q + (4 + 3 * e))
                            dve.tensor_copy(actT[0].rearrange("p c n -> p (c n)"), bank[6][:, :]).then_inc(ov_dve[l], 1)
                        dve.wait_ge(ov_pe[l], q + 14)
                        y_out_gated(l, ov_dve[l], 1)
                        dve.wait_ge(ov_pe[l], q + 15)
                        for k in range(4):
                            ins = add_x(k, bank[k])
                        ins.then_inc(ov_dve[l], 1)
                    dve.wait_ge(ov_dve[l], 52)

            dve.wait_ge(dist_i, 2)
            for k, d in ((2, 4), (3, 16)):
                rem = view(0, 256).bitcast(I32)
                step(dve.tensor_single_scalar(rem, idx[:, :], d - 1, ALU.bitwise_and))
                step(dve.tensor_copy(view(256, 256), rem))
                step(dve.tensor_scalar(view(256, 256), view(256, 256), 1.0, BIG, ALU.min, ALU.mult))
                dve.scalar_tensor_tensor(out=dist[:, k, :], in0=dist[:, 0, :], scalar=1.0 / d, in1=view(256, 256),
                                         op0=ALU.mult, op1=ALU.add).then_inc(dist_done, 1)
                dve.wait_ge(dist_done, k - 1)
            dve.wait_ge(turn_full, 1)
            dve.memset(qz[0][64:128, :, :], 0.0)
            dve.memset(qz[1][0:64, :, :], 0.0).then_inc(qz_zero, 1)
            dve.wait_ge(consts, 5)
            dve.wait_ge(cact_ready, 1)
            ada_static([0, 1, 2, 3])
            open_phase(0)
            norm(0)
            even()
            ada_static(range(6, 12))
            open_phase(1)
            norm(1)
            dve.wait_ge(rb_in, 16)
            route(0)
            experts(0)
            dve.wait_ge(tail_free, 8)
            overflow(0)
            open_phase(2)
            norm(2)
            odd()
            open_phase(3)
            norm(3)
            route(1)
            experts(1)
            dve.wait_ge(tail_free, 16)
            overflow(1)
            dve.memset(stat[:, 0:1], 0.0).then_inc(x_ready, 1)
            rstd_of(4)
            dve.wait_ge(pow_done, NORM_ROOT[4])
            dve.wait_ge(fg_in, 16)
            for t in range(T):
                dve.scalar_tensor_tensor(out=xh[:, t, :], in0=xs[:, t, :], scalar=rstd[:, t:t + 1], in1=fgrow,
                                         op0=ALU.mult, op1=ALU.mult).then_inc(final_ready, 1)


def kernel(x, c, norm1_g, norm2_g, ada_w, ada_b, ev_w_in, ev_w_out, sgu_ln_g, sgu_ln_b, sgu_w, sgu_b, lam_q1, lam_k1,
           lam_q2, lam_k2, diff_subln_g, od_w_in, od_w_out, conv_w, conv_b, conv_ln_g, conv_ln_b, router_w, router_b,
           moe_w_gu, moe_w_down, final_g):
    import numpy as np
    import concourse.bacc as bacc
    from concourse.bass_utils import run_bass_kernel_spmd

    def by_partition(a):
        a = np.asarray(a)
        a = a.reshape(-1, a.shape[-1] // P, P)
        return a.transpose(2, 0, 1).reshape(P, -1)

    n1, n2 = np.asarray(norm1_g), np.asarray(norm2_g)
    cols = np.concatenate([
        by_partition(c), by_partition(np.stack([n1[0], n2[0], n1[1], n2[1]])), by_partition(ada_b),
        by_partition(conv_b), by_partition(conv_ln_g), by_partition(conv_ln_b),
        np.asarray(conv_w)[0].reshape(TAPS, 4, P).transpose(2, 1, 0).reshape(P, -1),
        np.asarray(sgu_b)[0].T,
        np.asarray(router_w).reshape(KC, P, 16).transpose(1, 0, 2).reshape(P, -1)], axis=1)
    rows = np.concatenate([np.asarray(a).reshape(-1) for a in (
        sgu_ln_g, sgu_ln_b, diff_subln_g, lam_q1, lam_k1, lam_q2, lam_k2, router_b)])[None]
    ab = np.asarray(ada_b)
    gate_b = np.concatenate([ab[0, 2 * D:3 * D], ab[0, 5 * D:6 * D], ab[1, 2 * D:3 * D], ab[1, 5 * D:6 * D]])
    arrays = {"x": np.asarray(x)[0], "cols": cols, "rows": rows, "gate_b": gate_b, "ada_w": ada_w,
              "ev_w_in": ev_w_in, "ev_w_out": ev_w_out, "sgu_w": sgu_w, "od_w_in": od_w_in, "od_w_out": od_w_out,
              "w_gu": moe_w_gu, "w_down": moe_w_down, "final_g": final_g}
    arrays = {f"{n}_dram": np.ascontiguousarray(a) for n, a in arrays.items()}
    nc = bacc.Bacc("TRN2", target_bir_lowering=False, num_devices=1)
    args = [nc.dram_tensor(n, a.shape, mybir.dt.from_np(a.dtype), kind="ExternalInput").ap() for n, a in arrays.items()]
    y = nc.dram_tensor("y_dram", (T * P, D), F32, kind="ExternalOutput").ap()
    trunk(nc, *args, y)
    r = run_bass_kernel_spmd(nc, [arrays], core_ids=[0])
    return r.results[0]["y_dram"].reshape(1, T * P, D)
```

```python
from contextlib import ExitStack

import concourse.bass as bass
from concourse import mybir

ALU = mybir.AluOpType
ACT = mybir.ActivationFunctionType
AX = mybir.AxisListType.X
F32 = mybir.dt.float32
F32R = mybir.dt.float32r
I32 = mybir.dt.int32

P = 128
D = 1024
KC = D // P
T = 2
CAP = 128
PANELS = 4
W = 512
BIG = 1e34
RMS_EPS, LN_EPS = 1e-6, 1e-5
LAM_INIT = 0.2
TAPS = 31

C_C, C_NG, C_ADAB, C_CONVB, C_CLG, C_CLB = 0, 8, 40, 136, 140, 144
C_CONVW = 148
C_SGUB = C_CONVW + 4 * TAPS
C_RW = C_SGUB + 4
C_ALL = C_RW + KC * 16
R_LNG, R_LNB, R_SUBG, R_LAM, R_RB = 0, 512, 1024, 1152, 1408
R_ALL = R_RB

EV_ORDER = [("v", 512), ("q", 1024), ("k", 1536), ("vd", 2048), ("u", 0)]
OD_ORDER = [("gate", 4096), ("a", 3584), ("v", 3072), ("q0", 0), ("k0", 1536), ("q1", 512), ("k1", 2048),
            ("q2", 1024), ("k2", 2560)]


ADA_STEPS = [0, 2, 4, 6]


def body_items(ada):
    out = []
    for n in range(8):
        out += [("G", n), ("U", n)] + ([("D", n - 1)] if n else [])
        if ada and n in ADA_STEPS:
            out.append(("A", ADA_STEPS.index(n)))
    return out + [("D", 7)]


PRE = [[("ada", 0), ("ada", 1), ("ada", 2), ("ada", 3), ("in", "v"), ("in", "q"), ("ada", 4), ("ada", 5), ("in", "k"),
        ("ada", 6), ("in", "vd"), ("ada", 7), ("ada", 8), ("in", "u"), ("ada", 9), ("ada", 10), ("ada", 11),
        ("out", 0), ("out", 1)],
       [("in", n) for n, _ in OD_ORDER[:7]] + [("ada", 8), ("in", "q2"), ("in", "k2"), ("ada", 9), ("ada", 10),
                                               ("ada", 11), ("out", 0), ("out", 1)]]
BODY = [body_items(True), body_items(False)]
PRE_AT = [0, len(PRE[0]) + 2 * len(BODY[0])]
BODY_AT = [PRE_AT[0] + len(PRE[0]), PRE_AT[1] + len(PRE[1])]
assert all(len(b) % PANELS == 0 for b in BODY)


class Place:

    def __init__(self, at, i=None, per=0):
        self.slot = at % PANELS
        rnd = at // PANELS
        self.landed = 16 * (rnd + 1) if i is None else i * (16 * per // PANELS) + 16 * (rnd + 1)
        self.done = rnd + 1 if i is None else i * (per // PANELS) + rnd + 1
        self.before = rnd if i is None else i * (per // PANELS) + rnd


def pre_place(l, item):
    return Place(PRE_AT[l] + PRE[l].index(item))


def body_place(l, item, i):
    return Place(BODY_AT[l] + BODY[l].index(item), i, len(BODY[l]))


class Turn:

    def __init__(self, per):
        self.per, self.n, self.i, self.l, self.at = per, 0, None, 0, 0

    def enter(self, l, i):
        self.l, self.i, self.at = l, i, self.n

    def leave(self):
        assert self.n - self.at == self.per[self.l], (self.n - self.at, self.per, self.l)
        self.n += self.per[self.l]
        self.i = None

    def value(self, k=0):
        return self.n + k if self.i is None else self.i * self.per[self.l] + (self.n + k)

    def tick(self):
        self.n += 1


QUARTER = 2 * W
PARTS = 4
TURN_PER = [10, 10]
MISC_PER = [14, 10]

NORM_ROOT = [1, 6, 7, 9, 10]

ATT_SEQ = ["S0", "S1", "F", "T0", "S2", "A0", "T1", "S3", "A1", "F", "T2", "S4", "A2", "T3", "S5", "A3", "F",
           "T4", "A4", "T5", "A5", "F"]


def att_fill(l, j):
    nh, nk, t = (4, P, 0) if j < 2 else (2, 2 * P, 1)
    if l == 0:
        h0 = 4 * j if t == 0 else 2 * (j - 2)
        return t, slice(h0, h0 + nh), nh, nk
    h0 = j if t == 0 else 4 * ((j - 2) // 2) + (j - 2) % 2
    return t, slice(h0, h0 + 2 * nh - 1, 2), nh, nk


def heads_of(s):
    return list(range(s.start, s.stop, s.step or 1))


def trunk(nc, x, cols, rows, router_b, ada_w, ev_w_in, ev_w_out, sgu_w, od_w_in, od_w_out, w_gu, w_down,
          final_g, out):
    ctx = ExitStack()
    with ctx:
        def sb(name, shape, dt=F32):
            return ctx.enter_context(nc.sbuf_tensor(name, shape, dt))

        def sem(name):
            return ctx.enter_context(nc.semaphore(name))

        ring = sb("ring", [P, PANELS, KC * W])
        xs = sb("xs", [P, T, D])
        xh = sb("xh", [P, T, D])
        hT = sb("hT", [P, KC, T * P])
        gb = sb("gb", [P, 2, D])
        col = sb("col", [P, C_ALL])
        ident = sb("ident", [P, P])
        ones = sb("ones", [P, P])
        tri = sb("tri", [P, P])
        slot_no = sb("slot_no", [P, P])
        slot_all = sb("slot_all", [P, P])
        dist = sb("dist", [P, 4, 2 * P])
        idx = sb("idx", [P, 2 * P], I32)
        small = sb("small", [P, 960])
        flag = sb("flag", [P, 2], I32)
        SCR = 12416
        scr = sb("scr", [P, SCR])
        bank = [ctx.enter_context(nc.psum_tensor(f"bank{b}", [P, 512], F32)) for b in range(8)]
        mixT = xh[:, :, :].rearrange("p t (a n) -> p (t a) n", n=2 * P)

        def panel(s):
            return ring[:, s, :].rearrange("p (c n) -> p c n", c=KC)

        def view(off, *dims, base=scr):
            n = 1
            for d in dims:
                n *= d
            v = base[:, off:off + n]
            if len(dims) == 2:
                v = v.rearrange("p (a b) -> p a b", a=dims[0])
            if len(dims) == 3:
                v = v.rearrange("p (a b c) -> p a b c", a=dims[0], b=dims[1])
            return v

        sm = lambda off, *dims: view(off, *dims, base=small)
        cact = sm(0, 8)
        ssq, rms_t, rstd = sm(8, 2), sm(10, 2), sm(12, 2)
        mod = sb("mod", [P, 2, 48])
        shift = lambda l, s, c: mod[:, l, 24 * s + c:24 * s + c + 1]
        scale = lambda l, s, c: mod[:, l, 24 * s + 8 + c:24 * s + 9 + c]
        nslope = sm(80, 2, 8)
        qscale = sm(96, 4)
        lamrow = sm(100, 8)
        lam_t = sm(108, 4)
        mx = sm(112, 2, 8)
        nm_ev = sm(128, 2, 8)
        den_ev = sm(144, 2, 8)
        rden = sm(160, 2, 8)
        nm_od = sm(176, 3, 16)
        den_od = sm(224, 3, 16)
        e_od = sm(272, 3, 16)
        w_od = sm(320, 3, 16)
        nmin = sm(368, 16)
        wsum = sm(384, 16)
        stat = sm(400, 12)
        mv = sm(412, 4)
        ms4 = sm(416, 8)
        lg = sm(424, 2, 16)
        pr = sm(456, 2, 16)
        sel = sm(488, 2, 16)
        s16 = sm(520, 2, 16)
        oh1 = sm(552, 2, 16)
        oh2 = sm(584, 2, 16)
        gates = sm(616, 2, 16)
        no16 = sm(648, 16)
        g4 = [sm(664 + 8 * k, 2, 4) for k in range(6)]
        oh = sm(712, 2, 4)
        rank = sm(720, 2, 4)
        rank2 = sm(728, 2, 4)
        one2 = [sm(736 + 2 * k, 2) for k in range(6)]
        gslot = sm(748, 2, 4)
        cnt = sm(756, 4)
        cmax = sm(760, 1)
        lam_p = sm(762, 2, 64)
        minus_half = sm(892, 1)

        qT = [view(0, 4, 256), view(1024, 4, 256)]
        kT = [view(2048, 4, 256), view(3072, 4, 256)]
        vv = view(4096, 2, 512)
        uu, vg, vn = view(5120, 2, 512), view(6144, 2, 512), view(7168, 2, 512)
        sc = [view(8192, 512), view(8704, 512)]
        pT = [view(9216, 512), view(9728, 512)]
        oo = view(10240, 512)
        row = view(10752, R_ALL)
        qz = [view(0, 4, 256), view(3072, 4, 256)]
        wT, sgw = view(1024, 4, 128), view(3072, 4, 128)
        acc_mixer = [gb[:, 0, 0:W], gb[:, 0, W:2 * W]]
        acc_experts = [view(7168, 512), view(7680, 512)]
        sg = gb[:, 1, :].rearrange("p (c n) -> p c n", c=4)
        glu = view(5120, 4, 286)
        conv = view(6272, 4, 256)
        sc_o = [view(7296, 512), view(7808, 512)]
        pT_o = [view(8320, 512), view(8832, 512)]
        og = view(9344, 3, 16, 64)
        pcur = [view(0, 2, 128), view(256, 2, 128)]
        pt = [view(512, 2, 128), view(768, 2, 128)]
        hg = [view(1024, 8, 128), view(2048, 8, 128)]
        sil = [view(3072, 512), view(3584, 512)]
        act_t = [view(4096, 512), view(4608, 512)]
        actT = [view(5120, 4, 128), view(5632, 4, 128)]
        ysb = view(6144, 1024)
        w_hi = sb("w_hi", [P, PARTS, QUARTER], F32R)
        w_lo = sb("w_lo", [P, PARTS, QUARTER], F32R)
        h_hi = sb("h_hi", [P, 2, KC, P], F32R)
        h_lo = sb("h_lo", [P, 2, KC, P], F32R)
        rb_row = sb("rb_row", [P, 16])
        fgrow = hT[:, 0:4, :].rearrange("p c n -> p (c n)")

        panel_in = [sem(f"panel_in{s}") for s in range(PANELS)]
        panel_done = [sem(f"panel_done{s}") for s in range(PANELS)]
        x_in, cols_in, rows_in, rb_in, fg_in, sguw_in = (sem(n) for n in (
            "x_in", "cols_in", "rows_in", "rb_in", "fg_in", "sguw_in"))
        out_sem = sem("out_stored")
        const_step, consts, dist_i, dist_done, sguw_masked = (sem(n) for n in (
            "const_step", "consts", "dist_i", "dist_done", "sguw_masked"))
        cact_ready = sem("cact_ready")
        ada_step = sem("ada_step")
        dve_step, act_step = sem("dve_step"), sem("act_step")
        x_ready, ssq_ready, pow_done, xh_ready, xT_ready = (sem(n) for n in (
            "x_ready", "ssq_ready", "pow_done", "xh_ready", "xT_ready"))
        hT_dve, hT_act = sem("hT_dve"), sem("hT_act")
        turn_full, turn_free = sem("turn_full"), sem("turn_free")
        misc_full, misc_free = sem("misc_full"), sem("misc_free")
        fill_done = [sem("fill_done0"), sem("fill_done1")]
        fill_act = [sem("fill_act0"), sem("fill_act1")]
        fill_dve = [sem("fill_dve0"), sem("fill_dve1")]
        score_done, score_out, p_ready, a_ready, lam_part = (sem(n) for n in (
            "score_done", "score_out", "p_ready", "a_ready", "lam_part"))
        lam_exp = sem("lam_exp")
        vn_ready, sgu_mixed, aout_ready, bout_ready = (sem(n) for n in (
            "vn_ready", "sgu_mixed", "aout_ready", "bout_ready"))
        sq_ready, conv_ready, xc_ready, xn_ready, dout_ready, ediff_ready, e_ready, cout_ready = (sem(n) for n in (
            "sq_ready", "conv_ready", "xc_ready", "xn_ready", "dout_ready", "ediff_ready", "e_ready", "cout_ready"))
        conv_step = sem("conv_step")
        lg_done, lgm_ready, pr_ready, oh_ready, rank_done, flag_ready = (sem(n) for n in (
            "lg_done", "lgm_ready", "pr_ready", "oh_ready", "rank_done", "flag_ready"))
        p_built, sil_ready, act_ready, y_out, tail_full, tail_free = (sem(n) for n in (
            "p_built", "sil_ready", "act_ready", "y_out", "tail_full", "tail_free"))
        ov_in = [sem(f"over_in{l}") for l in range(2)]
        ov_pe = [sem(f"over_pe{l}") for l in range(2)]
        ov_dve = [sem(f"over_dve{l}") for l in range(2)]
        ov_act = [sem(f"over_act{l}") for l in range(2)]
        final_ready = sem("final_ready")
        hi_ready, lo_ready, part_used = sem("hi_ready"), sem("lo_ready"), sem("part_used")
        h_hi_act, h_hi_dve, h_ready = sem("h_hi_act"), sem("h_hi_dve"), sem("h_ready")
        pow_asked = sem("pow_asked")
        half_step = sem("half_step")
        qz_zero = sem("qz_zero")
        diag_ready = sem("diag_ready")

        ada_v = [ada_w[l].rearrange("(c p) (s j m) -> s j p c m", p=P, s=3, m=W) for l in range(2)]
        ev_v = ev_w_in[0].rearrange("(c p) m -> p c m", p=P)
        od_v = od_w_in[0].rearrange("(c p) m -> p c m", p=P)
        out_v = [w[0].rearrange("(c p) m -> p c m", p=P) for w in (ev_w_out, od_w_out)]
        gu_v = [w_gu[l].rearrange("e (c p) (h f) -> h e p c f", p=P, h=2) for l in range(2)]
        dn_v = [w_down[l].rearrange("e (c p) m -> e p c m", p=P) for l in range(2)]

        def down_panel(s):
            return ring[:, s, :].rearrange("p (c m) -> p c m", c=4)

        def quarter(n, kind, q):
            return 4 * (2 * n + (kind == "U")) + q

        def hi_at(l, i, k):
            return i * 64 + (128 * l + k + 1)

        def used_at(l, i, k):
            return i * 64 + (128 * l + k + 1 + PARTS)

        def lo_at(l, i, k):
            return i * 48 + (96 * l + 3 * (k // 4) + k % 4 + 1)

        def raw_quarter(pl, q):
            return ring[:, pl.slot, q * QUARTER:(q + 1) * QUARTER]

        FILLS = [[("in", n, h) for n, _ in EV_ORDER for h in range(2)] + [("out", j, t) for j in range(2) for t in range(2)],
                 [("in", n, h) for n, _ in OD_ORDER for h in range(2)] + [("out", j, t) for j in range(2) for t in range(2)]]
        DVE_EMPTIES = [{"k", "vd", 0, 1}, {"a", 0, 1}]

        def emptied(l, f):
            mine = FILLS[l][f][1] in DVE_EMPTIES[l]
            n = sum((FILLS[l][g][1] in DVE_EMPTIES[l]) == mine for g in range(f + 1))
            return (fill_dve if mine else fill_act)[l], n

        def wait_fill(eng, l, f):
            kind, name, h = FILLS[l][f]
            if h == 1:
                pl = pre_place(l, (kind, name))
                eng.wait_ge(panel_done[pl.slot], pl.done)
            else:
                eng.wait_ge(fill_done[l], f // 2 + 1)

        def fill_bank(f):
            return bank[f % 4]

        block = ctx.enter_context(nc.Block())

        @block.sync
        def _(sp):
            def load(pl, dst, src, wait):
                if wait:
                    sp.wait_ge(panel_done[pl.slot], pl.before)
                sp.dma_start(dst, src).then_inc(panel_in[pl.slot], 16)

            def load_pre(l):
                offs = dict(EV_ORDER if l == 0 else OD_ORDER)
                for k, (kind, n) in enumerate(PRE[l]):
                    pl = Place(PRE_AT[l] + k)
                    if kind == "ada":
                        src = ada_v[l][n // 4, n % 4]
                    elif kind == "in":
                        src = (ev_v if l == 0 else od_v)[:, :, offs[n]:offs[n] + W]
                    else:
                        src = out_v[l][:, :, n * W:(n + 1) * W]
                    load(pl, panel(pl.slot), src, PRE_AT[l] + k >= PANELS)

            def load_body(l):
                with sp.Fori(0, 2) as i:
                    for k, (kind, n) in enumerate(BODY[l]):
                        pl = Place(BODY_AT[l] + k, i, len(BODY[l]))
                        if kind == "A":
                            load(pl, panel(pl.slot), ada_v[1][i, n], True)
                        elif kind == "D":
                            load(pl, down_panel(pl.slot), dn_v[l][i * 8 + n], True)
                        else:
                            load(pl, panel(pl.slot), gu_v[l][0 if kind == "G" else 1, i * 8 + n], True)

            def overflow(l):
                sp.wait_ge(flag_ready, l + 1)
                over = sp.value_load(flag[0:1, l:l + 1])
                with sp.If(over > 0):
                    end = BODY_AT[l] + 2 * len(BODY[l])
                    for at in range(end - PANELS, end):
                        sp.wait_ge(panel_done[at % PANELS], at // PANELS + 1)
                    with sp.Fori(0, 4) as g:
                        for e in range(4):
                            sp.wait_ge(ov_pe[l], g * 15 + (1 if e == 0 else 2 + 3 * e))
                            sp.dma_start(panel(0), gu_v[l][0, g * 4 + e]).then_inc(ov_in[l], 16)
                            sp.dma_start(panel(1), gu_v[l][1, g * 4 + e]).then_inc(ov_in[l], 16)
                            sp.dma_start(down_panel(2), dn_v[l][g * 4 + e]).then_inc(ov_in[l], 16)
                    sp.wait_ge(ov_pe[l], 60)

            sp.dma_start(col[:, :], cols).then_inc(cols_in, 16)
            for l in range(2):
                load_pre(l)
                load_body(l)
                overflow(l)

        @block.gpsimd
        def _(pool):
            pool.memset(ones[:, :], 1.0).then_inc(const_step, 1)
            pool.memset(ident[:, :], 0.0).then_inc(const_step, 1)
            pool.wait_ge(const_step, 2)
            pool.affine_select(out=ident[:, :], in_=ident[:, :], compare_op=ALU.not_equal, fill=1.0, base=0,
                               pattern=[[-1, P]], channel_multiplier=1).then_inc(consts, 1)
            pool.affine_select(out=tri[:, :], in_=ones[:, :], compare_op=ALU.is_gt, fill=0.0, base=0,
                               pattern=[[1, P]], channel_multiplier=-1).then_inc(consts, 1)
            pool.iota(slot_all[:, :], [[1, P]], base=0, channel_multiplier=0,
                      allow_small_or_imprecise_dtypes=True).then_inc(const_step, 1)
            pool.wait_ge(const_step, 3)
            pool.affine_select(out=slot_no[:, :], in_=slot_all[:, :], compare_op=ALU.is_gt, fill=-1.0, base=CAP,
                               pattern=[[-1, P]], channel_multiplier=0).then_inc(consts, 1)
            pool.iota(no16, [[1, 16]], base=0, channel_multiplier=0,
                      allow_small_or_imprecise_dtypes=True).then_inc(consts, 1)
            for v in range(8):
                ins = pool.memset(nslope[:, 0, v:v + 1], -(2.0 ** (-2 * (v // 2 + 1))))
                if v == 0:
                    ins.then_inc(part_used, PARTS)
                last = pool.memset(nslope[:, 1, v:v + 1], -(2.0 ** -(v + 1)))
            last.then_inc(half_step, 1)
            for c in range(4):
                pool.wait_ge(half_step, 2 * c + 1)
                pool.memset(qscale[:, c:c + 1], 0.125 * 2.0 ** (2 * c + 2)).then_inc(half_step, 1)
                pool.wait_ge(half_step, 2 * c + 2)
                pool.memset(qscale[0:64, c:c + 1], 0.125 * 2.0 ** (2 * c + 1)).then_inc(half_step, 1)
            pool.wait_ge(half_step, 9)
            pool.memset(minus_half, -0.5).then_inc(consts, 1)
            pool.iota(idx[:, :], [[-1, 2 * P]], base=P + 256, channel_multiplier=1).then_inc(dist_i, 1)
            pool.iota(dist[:, 1, :], [[-1, 2 * P]], base=P, channel_multiplier=1,
                      allow_small_or_imprecise_dtypes=True).then_inc(const_step, 1)
            pool.wait_ge(const_step, 4)
            pool.affine_select(out=dist[:, 0, :], in_=dist[:, 1, :], compare_op=ALU.is_ge, fill=BIG, base=P,
                               pattern=[[-1, 2 * P]], channel_multiplier=1).then_inc(const_step, 1)
            pool.wait_ge(const_step, 5)
            pool.affine_select(out=dist[:, 1, :], in_=dist[:, 0, :], compare_op=ALU.is_ge, fill=BIG, base=0,
                               pattern=[[1, 2 * P]], channel_multiplier=-1).then_inc(dist_i, 1)
            pool.wait_ge(sguw_in, 16)
            pool.affine_select(out=sgw, in_=sgw, compare_op=ALU.is_ge, fill=0.0, base=0,
                               pattern=[[0, 4], [-1, P]], channel_multiplier=1).then_inc(sguw_masked, 1)
            roots = [(rstd, rms_t), (mv[:, 2:3], mv[:, 3:4]), (mv[:, 2:3], mv[:, 3:4]),
                     (ms4[:, 4:8], ms4[:, 0:4]), (ms4[:, 4:8], ms4[:, 0:4]), (rstd, rms_t), (rstd, rms_t),
                     (mv[:, 2:4], mv[:, 0:2]), (rstd, rms_t), (rstd, rms_t)]

            def root(n):
                to, of = roots[n]
                pool.wait_ge(pow_asked, n + 1)
                pool.tensor_tensor(to, of, minus_half.to_broadcast([P, of.shape[1]]), ALU.pow).then_inc(pow_done, 1)

            for n in range(9):
                root(n)
            pool.wait_ge(flag_ready, 2)
            pool.dma_start(fgrow, final_g.partition_broadcast(P)).then_inc(fg_in, 16)
            root(9)

        @block.tensor
        def _(pe):
            turn, misc = Turn(TURN_PER), Turn(MISC_PER)

            def take(which):
                sems = turn_free if which is turn else misc_free
                if which.n or which.i is not None:
                    pe.wait_ge(sems, which.value())

            def give(which, ins):
                ins.then_inc(turn_full if which is turn else misc_full, 1)
                which.tick()

            def transposes(blocks, which=None, rows_=P):
                which = which or turn
                b = bank[6] if which is turn else bank[7]
                take(which)
                for k, src in enumerate(blocks):
                    ins = pe.transpose(b[:, k * P:(k + 1) * P], src, ident[:, :])
                give(which, ins)

            def norm_T(ph):
                pe.wait_ge(xh_ready, 2 * (ph + 1))
                for b in range(4):
                    for k in range(4):
                        c, t = 2 * b + k // 2, k % 2
                        ins = pe.transpose(bank[b][:, k * P:(k + 1) * P], xh[:, t, c * P:(c + 1) * P], ident[:, :])
                    ins.then_inc(xT_ready, 1)
                pe.wait_ge(hT_dve, 4 * (ph + 1))
                pe.wait_ge(hT_act, 4 * (ph + 1))

            def ada_sum(acc, a, pl):
                take(misc)
                pe.wait_ge(panel_done[pl.slot], pl.done)
                for m in range(4):
                    ins = pe.matmul(bank[7][:, m:m + 1], acc[a][:, m * P:(m + 1) * P], ones[:, 0:1],
                                    start=True, stop=True)
                give(misc, ins)

            def gate_rows(l):
                for s in range(2):
                    for h in range(2):
                        take(misc)
                        for m in range(4):
                            c = 24 * s + 16 + 4 * h + m
                            ins = pe.matmul(bank[7][:, m * P:(m + 1) * P], mod[:, l, c:c + 1].to_broadcast([P, P]),
                                            ident[:, :], start=True, stop=True)
                        give(misc, ins)

            def fill(l, f):
                kind, name, h = FILLS[l][f]
                pl = pre_place(l, (kind, name))
                if f >= 4:
                    pe.wait_ge(*emptied(l, f - 4))
                if h == 0:
                    pe.wait_ge(panel_in[pl.slot], pl.landed)
                w, b = panel(pl.slot), fill_bank(f)
                if kind == "out":
                    for c in range(KC):
                        ins = pe.matmul(b[:, :], mixT[:, c, h * P:(h + 1) * P], w[:, c, :],
                                        start=(c == 0), stop=(c == KC - 1))
                elif name in ("v", "u", "vd"):
                    for c in range(KC):
                        ins = pe.matmul(b[:, :], hT[:, c, h * P:(h + 1) * P], w[:, c, :],
                                        start=(c == 0), stop=(c == KC - 1))
                else:
                    for m in range(2):
                        for c in range(KC):
                            ins = pe.matmul(b[:, m * 256:(m + 1) * 256], w[:, c, (2 * h + m) * P:(2 * h + m + 1) * P],
                                            hT[:, c, :], start=(c == 0), stop=(c == KC - 1))
                if h == 1:
                    ins.then_inc(panel_done[pl.slot], 1)
                else:
                    ins.then_inc(fill_done[l], 1)

            def attention(l, g, between):
                base = 6 * (g if l == 0 else g + 1)
                q, k = qT[g % 2], kT[g % 2]
                s_, p_ = (sc, pT) if l == 0 else (sc_o, pT_o)
                todo = list(between)
                for step in ATT_SEQ:
                    if step == "F":
                        if todo:
                            for f in todo.pop(0):
                                f()
                        continue
                    j = int(step[1])
                    n = base + j
                    t, hs, nh, nk = att_fill(l, j)
                    if step[0] == "S":
                        if n >= 2:
                            pe.wait_ge(score_out, n - 1)
                        for v, h in enumerate(heads_of(hs)):
                            if l == 0:
                                q, r = qz[h % 2], slice(0, P)
                            else:
                                r = slice(64 * (h % 2), 64 * (h % 2) + 64)
                            ins = pe.matmul(bank[4 + n % 2][:, v * nk:(v + 1) * nk],
                                            q[r, h // 2, t * P:(t + 1) * P], k[r, h // 2, 0:nk],
                                            start=True, stop=True)
                        ins.then_inc(score_done, 1)
                    elif step[0] == "T":
                        pe.wait_ge(*((a_ready, n + 1) if l == 0 else (p_ready, n + 1)))
                        if l == 0:
                            blocks = [s_[n % 2][:, o:o + P] for o in ((0, 2 * P) if t == 0 else (0, P))]
                        else:
                            blocks = [s_[n % 2][:, o * P:(o + 1) * P] for o in range(4)]
                        transposes(blocks)
                    else:
                        if j in (0, 2):
                            take(misc)
                            if l == 0 and j == 0:
                                pe.wait_ge(*emptied(0, 7))
                        pe.wait_ge(turn_free, at_turn[n])
                        nb = t + 1
                        heads = [h // 2 for h in heads_of(hs)][::2] if l == 0 else heads_of(hs)
                        wd = P if l == 0 else 64
                        for v, h in enumerate(heads):
                            for kb in range(nb):
                                ins = pe.matmul(bank[7][:, h * wd:(h + 1) * wd],
                                                p_[n % 2][:, (v * nb + kb) * P:(v * nb + kb + 1) * P],
                                                vv[:, kb, h * wd:(h + 1) * wd],
                                                start=(kb == 0), stop=(kb == nb - 1))
                        if j in (1, 5):
                            give(misc, ins)
                    if step[0] == "T":
                        at_turn[n] = turn.n

            at_turn = {}

            def even():
                base = 0
                ada = lambda j: ada_sum(acc_mixer, j % 2, pre_place(0, ("ada", j)))
                for f in range(4):
                    fill(0, f)
                ada(4)
                ada(5)
                for f in (4, 5):
                    fill(0, f)
                ada(6)
                pe.wait_ge(*emptied(0, 3))
                pe.wait_ge(qz_zero, 1)
                pe.wait_ge(*emptied(0, 5))
                attention(0, 0, [[lambda: (fill(0, 6), fill(0, 7), ada(7), ada(8))],
                                 [lambda: (fill(0, 8), ada(9))], [lambda: fill(0, 9)]])
                ada(10)
                ada(11)
                gate_rows(0)
                pe.wait_ge(score_out, 6)
                pe.wait_ge(vn_ready, 2)
                for t in range(T):
                    for g in range(4):
                        ins = pe.matmul(bank[4 + t][:, g * P:(g + 1) * P], wT[:, g, :], vn[:, t, g * P:(g + 1) * P],
                                        start=True, stop=True)
                    ins.then_inc(sgu_mixed, 1)
                for t in range(T):
                    pe.wait_ge(aout_ready, t + 1)
                    transposes([uu[:, t, c * P:(c + 1) * P] for c in range(4)])
                for t in range(T):
                    pe.wait_ge(bout_ready, t + 1)
                    transposes([vg[:, t, c * P:(c + 1) * P] for c in range(4)])
                pe.wait_ge(turn_free, turn.n)
                for f in range(10, 14):
                    fill(0, f)

            def odd():
                for f in range(10):
                    fill(1, f)
                pe.wait_ge(*emptied(1, 9))
                F = lambda f: (lambda: fill(1, f))

                def conv_sums():
                    take(misc)
                    pe.wait_ge(conv_ready, 1)
                    for c in range(4):
                        ins = pe.matmul(bank[7][:, 0:256], ones[:, :], conv[:, c, :], start=(c == 0), stop=(c == 3))
                    give(misc, ins)

                def conv_squares():
                    take(misc)
                    pe.wait_ge(sq_ready, 1)
                    for t in range(T):
                        for c in range(4):
                            ins = pe.matmul(bank[7][:, t:t + 1], sg[:, c, t * P:(t + 1) * P], ones[:, 0:1],
                                            start=(c == 0), stop=(c == 3))
                    give(misc, ins)

                def conv_rows():
                    take(misc)
                    pe.wait_ge(diag_ready, 1)
                    ins = pe.matmul(bank[7][:, 0:256], ones[:, :], sg[:, 0, :], start=True, stop=True)
                    give(misc, ins)

                ada = lambda j: (lambda: ada_sum(acc_mixer, j % 2, pre_place(1, ("ada", j))))
                attention(1, 0, [[F(10)], [F(11)], [F(12)], [F(13)]])
                conv_sums()
                ada(8)()
                pe.wait_ge(*emptied(1, 13))
                attention(1, 1, [[conv_squares, F(14)], [conv_rows, F(15), ada(9)], [F(16)],
                                 [F(17), ada(10), ada(11)]])
                pe.wait_ge(*emptied(1, 17))
                attention(1, 2, [])
                for t in range(T):
                    pe.wait_ge(cout_ready, 1)
                    transposes([qT[0].rearrange("p a b -> p (a b)")[:, t * 512 + c * P:t * 512 + (c + 1) * P]
                                for c in range(4)])
                gate_rows(1)
                pe.wait_ge(turn_free, turn.n)
                pe.wait_ge(dout_ready, 4)
                for f in range(18, 22):
                    fill(1, f)

            def route(l):
                take(misc)
                for t in range(T):
                    for c in range(KC):
                        ins = pe.matmul(bank[7][:, t * 16:(t + 1) * 16], hT[:, c, t * P:(t + 1) * P],
                                        col[:, C_RW + c * 16:C_RW + (c + 1) * 16], start=(c == 0), stop=(c == KC - 1))
                give(misc, ins)
                take(misc)
                pe.wait_ge(oh_ready, l + 1)
                pe.matmul(bank[7][:, 0:4], tri[:, :], oh[:, 0, :], start=True, stop=True)
                pe.matmul(bank[7][:, 4:8], ones[:, :], oh[:, 0, :], start=True, stop=False)
                pe.matmul(bank[7][:, 4:8], tri[:, :], oh[:, 1, :], start=False, stop=True)
                pe.matmul(bank[7][:, 8:12], ones[:, :], oh[:, 0, :], start=True, stop=False)
                ins = pe.matmul(bank[7][:, 8:12], ones[:, :], oh[:, 1, :], start=False, stop=True)
                give(misc, ins)

            def slot_gates(gg, g):
                take(misc)
                for t in range(T):
                    ins = pe.matmul(bank[7][:, 0:4], pcur[gg][:, t, :], gates[:, t, bass.ds(g * 4, 4)],
                                    start=(t == 0), stop=(t == T - 1))
                give(misc, ins)

            def gather(gg, half):
                which, b = ((turn, bank[6]), (misc, bank[7]))[half]
                take(which)
                for c in range(4):
                    cc = 4 * half + c
                    for t in range(T):
                        ins = pe.matmul(b[:, c * P:(c + 1) * P], xh[:, t, cc * P:(cc + 1) * P], pcur[gg][:, t, :],
                                        start=(t == 0), stop=(t == T - 1))
                give(which, ins)

            def scatter(gg, k, b):
                t, h = k // 2, k % 2
                return pe.matmul(b[:, :], pt[gg][:, t, :], ysb[:, h * W:(h + 1) * W], start=True, stop=True)

            def experts(l):
                with pe.Fori(0, 2) as i:
                    turn.enter(l, i)
                    misc.enter(l, i)
                    n0 = 16 * l
                    pe.wait_ge(p_built, i * 2 + (4 * l + 1))
                    slot_gates(0, i * 2)
                    gather(0, 0)
                    gather(0, 1)
                    act_at = {}

                    def up(n, kind):
                        b = bank[2 * (n % 2) + (kind == "U")]
                        pl = body_place(l, (kind, n), i)
                        if n >= 2:
                            pe.wait_ge(sil_ready if kind == "G" else act_ready, i * 8 + (n0 + n - 1))
                        for q in range(4):
                            k = quarter(n, kind, q)
                            hi, lo = (w[:, k % PARTS, :].rearrange("p (c n) -> p c n", c=2) for w in (w_hi, w_lo))
                            pe.wait_ge(hi_ready, hi_at(l, i, k))
                            for c in range(2):
                                pe.matmul(b[:, :], h_hi[:, n // 4, 2 * q + c, :], hi[:, c, :], start=(q == 0 and c == 0), stop=False)
                                pe.matmul(b[:, :], h_lo[:, n // 4, 2 * q + c, :], hi[:, c, :], start=False, stop=False)
                            if q < 3:
                                pe.wait_ge(lo_ready, lo_at(l, i, k))
                            else:
                                pe.wait_ge(panel_done[pl.slot], pl.done)
                            for c in range(2):
                                ins = pe.matmul(b[:, :], h_hi[:, n // 4, 2 * q + c, :], lo[:, c, :], start=False, stop=(q == 3 and c == 1))
                            ins.then_inc(part_used, 1)

                    def act_T(n):
                        pe.wait_ge(act_ready, i * 8 + (n0 + n + 1))
                        transposes([act_t[n % 2][:, c * P:(c + 1) * P] for c in range(4)])
                        act_at[n] = turn.value()

                    def down(n):
                        pl = body_place(l, ("D", n), i)
                        pe.wait_ge(panel_in[pl.slot], pl.landed)
                        pe.wait_ge(turn_free, act_at[n])
                        if n == 4:
                            pe.wait_ge(y_out, i * 2 + (4 * l + 1))
                        w = down_panel(pl.slot)
                        for c in range(4):
                            for h in range(2):
                                ins = pe.matmul(bank[4 + h][:, :], actT[n % 2][:, c, :], w[:, c, h * W:(h + 1) * W],
                                                start=(n % 4 == 0 and c == 0), stop=(n % 4 == 3 and c == 3),
                                                skip_group_check=True)
                        ins.then_inc(panel_done[pl.slot], 1)

                    def misc_scatter(k):
                        take(misc)
                        pe.wait_ge(y_out, i * 2 + (4 * l + 1))
                        give(misc, scatter(0, k, bank[7]))

                    for n in range(8):
                        if n in (0, 4):
                            pe.wait_ge(h_ready, i * 4 + (8 * l + 2 * (n // 4) + 2))
                        up(n, "G")
                        if n >= 1:
                            act_T(n - 1)
                        if n == 0:
                            transposes([pcur[0][:, t, :] for t in range(T)], misc)
                        if n == 2:
                            pe.wait_ge(p_built, i * 2 + (4 * l + 2))
                            slot_gates(1, i * 2 + 1)
                            gather(1, 0)
                        if n in (5, 6):
                            misc_scatter(0 if n == 5 else 3)
                        up(n, "U")
                        if n == 2:
                            gather(1, 1)
                        if n == 3:
                            transposes([pcur[1][:, t, :] for t in range(T)], misc)
                        if n == 5:
                            misc_scatter(1)
                        if n >= 1:
                            down(n - 1)
                        if l == 0 and n - 1 in ADA_STEPS:
                            a = ADA_STEPS.index(n - 1)
                            ada_sum(acc_experts, a % 2, body_place(0, ("A", a), i))
                        if n == 5:
                            misc_scatter(2)
                    act_T(7)
                    down(7)
                    pe.wait_ge(y_out, i * 2 + (4 * l + 2))
                    for k in range(4):
                        scatter(1, k, bank[k]).then_inc(tail_full, 1)
                    turn.leave()
                    misc.leave()

            def overflow(l):
                pe.wait_ge(flag_ready, l + 1)
                over = pe.value_load(flag[0:1, l:l + 1])
                with pe.If(over > 0):
                    pe.wait_ge(tail_free, 8 * (l + 1))
                    with pe.Fori(0, 4) as g:
                        d, q = g * 13, g * 4
                        pe.wait_ge(ov_dve[l], d + 1)
                        for t in range(T):
                            pe.transpose(bank[7][:, t * P:(t + 1) * P], pcur[0][:, t, :], ident[:, :])
                        for t in range(T):
                            ins = pe.matmul(bank[7][:, 256:260], pcur[0][:, t, :], gates[:, t, bass.ds(g * 4, 4)],
                                            start=(t == 0), stop=(t == T - 1))
                        ins.then_inc(ov_pe[l], 1)
                        pe.wait_ge(ov_dve[l], d + 2)
                        for cc in range(KC):
                            for t in range(T):
                                ins = pe.matmul(bank[6 + cc // 4][:, (cc % 4) * P:(cc % 4 + 1) * P],
                                                xh[:, t, cc * P:(cc + 1) * P], pcur[0][:, t, :],
                                                start=(t == 0), stop=(t == T - 1))
                        ins.then_inc(ov_pe[l], 1)
                        pe.wait_ge(ov_dve[l], d + 3)
                        for e in range(4):
                            pe.wait_ge(ov_in[l], g * 192 + 48 * (e + 1))
                            for k in range(2):
                                for c in range(KC):
                                    ins = pe.matmul(bank[k][:, :], hg[0][:, c, :], panel(k)[:, c, :],
                                                    start=(c == 0), stop=(c == KC - 1))
                            ins.then_inc(ov_pe[l], 1)
                            pe.wait_ge(ov_dve[l], d + (4 + 2 * e))
                            for c in range(4):
                                ins = pe.transpose(bank[6][:, c * P:(c + 1) * P], act_t[0][:, c * P:(c + 1) * P], ident[:, :])
                            ins.then_inc(ov_pe[l], 1)
                            pe.wait_ge(ov_dve[l], d + (5 + 2 * e))
                            for c in range(4):
                                for h in range(2):
                                    ins = pe.matmul(bank[4 + h][:, :], actT[0][:, c, :],
                                                    down_panel(2)[:, c, h * W:(h + 1) * W],
                                                    start=(e == 0 and c == 0), stop=(e == 3 and c == 3),
                                                    skip_group_check=True)
                            ins.then_inc(ov_pe[l], 1)
                        pe.wait_ge(ov_dve[l], d + 12)
                        for k in range(4):
                            ins = scatter(0, k, bank[k])
                        ins.then_inc(ov_pe[l], 1)
                        pe.wait_ge(ov_dve[l], d + 13)
                    pe.wait_ge(ov_dve[l], 52)

            pe.wait_ge(consts, 2)
            for j in range(4):
                ada_sum(acc_mixer, j % 2, pre_place(0, ("ada", j)))
            norm_T(0)
            pe.wait_ge(sguw_masked, 1)
            transposes([sgw[:, g, :] for g in range(4)])
            even()
            norm_T(1)
            route(0)
            experts(0)
            overflow(0)
            norm_T(2)
            odd()
            norm_T(3)
            route(1)
            experts(1)
            overflow(1)

        @block.scalar
        def _(act):
            turn = Turn(TURN_PER)
            steps = [0]

            def turn_copy(dst, n):
                act.wait_ge(turn_full, turn.value(1))
                turn.tick()
                act.activation(dst, n, ACT.Copy).then_inc(turn_free, 1)

            def norm(ph):
                if ph == 0:
                    act.wait_ge(x_in, 16)
                else:
                    act.wait_ge(x_ready, ph + 1)
                for t in range(T):
                    act.activation(xh[:, t, :], xs[:, t, :], ACT.Square, accum_out=ssq[:, t:t + 1])\
                       .then_inc(ssq_ready, 1)
                if ph == 4:
                    return
                act.wait_ge(pow_done, NORM_ROOT[ph])
                for t in range(T):
                    act.activation(xh[:, t, :], xs[:, t, :], ACT.Copy, scale=rstd[:, t:t + 1]).then_inc(xh_ready, 1)
                l, s = ph // 2, ph % 2
                if ph == 0:
                    act.wait_ge(x_ready, 1)
                for c in range(4, 8):
                    act.wait_ge(xT_ready, 4 * ph + c // 2 + 1)
                    act.activation(hT[:, c, :], bank[c // 2][:, 256 * (c % 2):256 * (c % 2) + 256], ACT.Identity,
                                   scale=scale(l, s, c), bias=shift(l, s, c)).then_inc(hT_act, 1)

            def exps(l, n, j, s_, nm, den):
                t, hs, nh, nk = att_fill(l, j)
                act.wait_ge(score_out, n + 1)
                for v, h in enumerate(heads_of(hs)):
                    slope = 2.0 ** (-2 * (h // 2 + 1)) if l == 0 else 2.0 ** -(h + 1)
                    o = s_[n % 2][:, v * nk:(v + 1) * nk]
                    ins = act.activation(o, o, ACT.Exp, scale=slope, bias=nm[:, h:h + 1], accum_out=den[:, h:h + 1])
                ins.then_inc(p_ready, 1)

            def attention(l, g, between):
                base = 6 * (g if l == 0 else g + 1)
                s_, p_ = (sc, pT) if l == 0 else (sc_o, pT_o)
                todo = list(between)
                for step in ATT_SEQ:
                    j = int(step[1]) if len(step) > 1 else 0
                    n, t = base + j, att_fill(l, j)[0]
                    if step == "F" and todo:
                        f = todo.pop(0)
                        empty_odd(f)
                    elif step[0] == "S":
                        if l == 0:
                            exps(l, n, j, s_, nm_ev[:, t, :], den_ev[:, t, :])
                        else:
                            exps(l, n, j, s_, nm_od[:, g, 8 * t:8 * t + 8], den_od[:, g, 8 * t:8 * t + 8])
                    elif step[0] == "T":
                        w = 2 * P if l == 0 else 4 * P
                        turn_copy(p_[n % 2][:, 0:w], bank[6][:, 0:w])

            def even():
                for h in range(2):
                    wait_fill(act, 0, h)
                    act.activation(vg[:, h, :], fill_bank(h)[:, :], ACT.Gelu_apprx_tanh).then_inc(fill_act[0], 1)
                for h in range(2):
                    wait_fill(act, 0, 2 + h)
                    for m in range(2):
                        c = 2 * h + m
                        for k in range(2):
                            r = slice(64 * k, 64 * k + 64)
                            ins = act.activation(qz[k][r, c, :], fill_bank(2 + h)[r, m * 256:(m + 1) * 256], ACT.Copy,
                                                 scale=0.125 * 4.0 ** (c + 1))
                    ins.then_inc(fill_act[0], 1)
                act.wait_ge(lam_part, 1)
                act.activation(lam_t[:, 2:4], lam_t[:, 0:2], ACT.Exp).then_inc(lam_exp, 1)
                attention(0, 0, [])
                for h in range(2):
                    wait_fill(act, 0, 8 + h)
                    act.activation(uu[:, h, :], fill_bank(8 + h)[:, :], ACT.Gelu_apprx_tanh).then_inc(fill_act[0], 1)
                for k in range(4):
                    t = k % 2
                    turn_copy(mixT[:, 4 * (k // 2):4 * (k // 2) + 4, t * P:(t + 1) * P],
                              bank[6][:, :].rearrange("p (c n) -> p c n", c=4))

            def empty_odd(f):
                _, name, h = FILLS[1][f]
                wait_fill(act, 1, f)
                b = fill_bank(f)
                if name == "gate":
                    ins = act.activation(sg[:, 2 * h:2 * h + 2, :], b[:, :].rearrange("p (c n) -> p c n", c=2), ACT.Sigmoid)
                elif name == "v":
                    ins = act.activation(vv[:, h, :], b[:, :], ACT.Copy)
                elif name[0] == "q":
                    for m in range(2):
                        c = 2 * h + m
                        ins = act.activation(qT[int(name[1]) % 2][:, c, :], b[:, m * 256:(m + 1) * 256], ACT.Copy,
                                             scale=qscale[:, c:c + 1])
                else:
                    ins = act.activation(kT[int(name[1]) % 2][:, 2 * h:2 * h + 2, :],
                                         b[:, :].rearrange("p (c n) -> p c n", c=2), ACT.Copy)
                ins.then_inc(fill_act[1], 1)

            def odd():
                for f in (0, 1, 4, 5, 6, 7, 8, 9):
                    empty_odd(f)
                attention(1, 0, [10, 11, 12, 13])
                act.wait_ge(xc_ready, 1)
                act.activation(sg, conv, ACT.Square).then_inc(sq_ready, 1)
                attention(1, 1, [14, 15, 16, 17])
                attention(1, 2, [])
                act.wait_ge(ediff_ready, 1)
                act.activation(e_od, e_od, ACT.Exp).then_inc(e_ready, 1)
                act.wait_ge(xn_ready, 1)
                for c in range(4):
                    act.activation(mixT[:, 4 + c, :], conv[:, c, :], ACT.Silu, scale=col[:, C_CLG + c:C_CLG + c + 1],
                                   bias=col[:, C_CLB + c:C_CLB + c + 1]).then_inc(dout_ready, 1)
                for t in range(T):
                    turn_copy(mixT[:, 0:4, t * P:(t + 1) * P], bank[6][:, :].rearrange("p (c n) -> p c n", c=4))

            def route(l):
                act.wait_ge(lgm_ready, l + 1)
                act.activation(pr, lg, ACT.Exp).then_inc(pr_ready, 1)

            def gather_cols(gg, l, half, b, src):
                for c in range(4):
                    cc = 4 * half + c
                    ins = act.activation(hg[gg][:, cc, :], src[:, c * P:(c + 1) * P], ACT.Identity,
                                         scale=scale(l, 1, cc), bias=shift(l, 1, cc))
                return ins

            def experts(l):
                with act.Fori(0, 2) as i:
                    turn.enter(l, i)
                    n0 = 16 * l

                    def gather(gg):
                        act.wait_ge(turn_full, turn.value(1))
                        turn.tick()
                        gather_cols(gg, l, 0, None, bank[6]).then_inc(turn_free, 1)
                        act.wait_ge(turn_free, turn.value())
                        act.activation(h_hi[:, gg, 0:4, :], hg[gg][:, 0:4, :], ACT.Copy).then_inc(h_hi_act, 1)

                    def act_T(n):
                        turn_copy(actT[n % 2], bank[6][:, :].rearrange("p (c n) -> p c n", c=4))

                    def split(n, kind):
                        pl = body_place(l, (kind, n), i)
                        act.wait_ge(panel_in[pl.slot], pl.landed)
                        for q in range(4):
                            k = quarter(n, kind, q)
                            act.wait_ge(part_used, used_at(l, i, k - PARTS))
                            act.activation(w_hi[:, k % PARTS, :], raw_quarter(pl, q), ACT.Copy).then_inc(hi_ready, 1)

                    split(0, "G")
                    gather(0)
                    for n in range(8):
                        split(n, "U")
                        if n >= 1:
                            act_T(n - 1)
                        act.wait_ge(part_used, used_at(l, i, quarter(n, "G", 3)))
                        if n >= 2:
                            act.wait_ge(act_ready, i * 8 + (n0 + n - 1))
                        act.activation(sil[n % 2], bank[2 * (n % 2)][:, :], ACT.Silu).then_inc(sil_ready, 1)
                        if n == 2:
                            gather(1)
                        if n < 7:
                            split(n + 1, "G")
                    act_T(7)
                    turn.leave()

            def overflow(l):
                act.wait_ge(flag_ready, l + 1)
                over = act.value_load(flag[0:1, l:l + 1])
                with act.If(over > 0):
                    with act.Fori(0, 4) as g:
                        for e in range(4):
                            act.wait_ge(ov_pe[l], g * 15 + (3 + 3 * e))
                            act.activation(sil[0], bank[0][:, :], ACT.Silu).then_inc(ov_act[l], 1)
                    act.wait_ge(ov_dve[l], 52)

            act.dma_start(xs[:, :, :], x.rearrange("(t p) d -> p t d", p=P)).then_inc(x_in, 16)
            act.dma_start(sgw, sgu_w[0].rearrange("g t s -> t g s")).then_inc(sguw_in, 16)
            act.dma_start(row, rows.partition_broadcast(P)).then_inc(rows_in, 16)
            act.dma_start(rb_row[:, :], router_b.partition_broadcast(P)).then_inc(rb_in, 16)
            act.wait_ge(cols_in, 16)
            act.wait_ge(consts, 5)
            act.activation(cact, col[:, C_C:C_C + 8], ACT.Silu).then_inc(cact_ready, 1)
            for l in range(2):
                norm(2 * l)
                if l == 0:
                    turn_copy(wT, bank[6][:, :].rearrange("p (c n) -> p c n", c=4))
                even() if l == 0 else odd()
                norm(2 * l + 1)
                route(l)
                experts(l)
                overflow(l)
            norm(4)
            act.wait_ge(final_ready, 2)
            act.dma_start(out.rearrange("(t p) d -> p t d", p=P), xh[:, :, :]).then_inc(out_sem, 16)
            act.wait_ge(out_sem, 16)

        @block.vector
        def _(dve):
            misc = Turn(MISC_PER)
            steps, turns_seen = [0], {}

            def step(ins):
                steps[0] += 1
                ins.then_inc(dve_step, 1)
                dve.wait_ge(dve_step, steps[0])

            def misc_in():
                dve.wait_ge(misc_full, misc.value(1))
                misc.tick()

            ada_n = [0]

            def ada_acc(acc, j, pl, i=None):
                a = acc[j % 2]
                dve.wait_ge(panel_in[pl.slot], pl.landed)
                w = panel(pl.slot)
                base = 7 * ada_n[0]
                ada_n[0] += 1
                dve.tensor_scalar(a, w[:, 0, :], cact[:, 0:1], None, ALU.mult).then_inc(ada_step, 1)
                for c in range(1, KC):
                    v = base + c
                    dve.wait_ge(ada_step, v if i is None else i * 28 + v)
                    ins = dve.scalar_tensor_tensor(out=a, in0=w[:, c, :], scalar=cact[:, c:c + 1], in1=a,
                                                   op0=ALU.mult, op1=ALU.add)
                    ins.then_inc(*((ada_step, 1) if c < KC - 1 else (panel_done[pl.slot], 1)))

            def ada_out(l, j):
                misc_in()
                o = bass.ds(j * 4, 4)
                bias = col[:, C_ADAB:C_ADAB + 96].rearrange("p (l k) -> p l k", l=2)
                dve.tensor_tensor(mod[:, l, o], bank[7][:, 0:4], bias[:, l, o], ALU.add).then_inc(misc_free, 1)

            def gates_out():
                for s in range(2):
                    for h in range(2):
                        misc_in()
                        dve.tensor_copy(gb[:, s, h * W:(h + 1) * W], bank[7][:, :]).then_inc(misc_free, 1)

            ada = lambda j: ada_acc(acc_mixer, j, pre_place(0, ("ada", j)))

            def open_phase(ph):
                l, s = ph // 2, ph % 2
                o = C_NG + 8 * (2 * l + s)
                dve.wait_ge(misc_free, misc.n)
                m = mod[:, l, 24 * s + 8:24 * s + 16]
                dve.scalar_tensor_tensor(out=m, in0=m, scalar=1.0,
                                         in1=col[:, o:o + 8], op0=ALU.add, op1=ALU.mult).then_inc(x_ready, 1)

            def distances():
                rem, away = oo[:, 0:256].bitcast(I32), oo[:, 256:512]
                for k, d in ((2, 4), (3, 16)):
                    step(dve.tensor_single_scalar(rem, idx[:, :], d - 1, ALU.bitwise_and))
                    step(dve.tensor_copy(away, rem))
                    step(dve.tensor_scalar(away, away, 1.0, BIG, ALU.min, ALU.mult))
                    dve.scalar_tensor_tensor(out=dist[:, k, :], in0=dist[:, 0, :], scalar=1.0 / d, in1=away,
                                             op0=ALU.mult, op1=ALU.add).then_inc(dist_done, 1)
                    dve.wait_ge(dist_done, k - 1)

            def rstd_of(ph):
                dve.wait_ge(ssq_ready, 2 * (ph + 1))
                dve.tensor_scalar(rms_t, ssq, 1.0 / D, RMS_EPS, ALU.mult, ALU.add).then_inc(pow_asked, 1)

            def norm(ph):
                rstd_of(ph)
                l, s = ph // 2, ph % 2
                dve.wait_ge(x_ready, ph + 1)
                for c in range(4):
                    dve.wait_ge(xT_ready, 4 * ph + c // 2 + 1)
                    dve.tensor_scalar(hT[:, c, :], bank[c // 2][:, 256 * (c % 2):256 * (c % 2) + 256],
                                      scale(l, s, c), shift(l, s, c),
                                      ALU.mult, ALU.add).then_inc(hT_dve, 1)

            def scores(l, n, j, s_, nm, d):
                t, hs, nh, nk = att_fill(l, j)
                dve.wait_ge(score_done, n + 1)
                if n >= 2 and (l == 0 or n >= 8):
                    dve.wait_ge(turn_full, at_turn_of(l, n - 2))
                o = s_[n % 2].rearrange("p (h k) -> p h k", h=nh)
                step(dve.tensor_tensor(o, bank[4 + n % 2][:, :].rearrange("p (h k) -> p h k", h=nh),
                                       dist[:, d:d + 1, 2 * P - nk:2 * P].to_broadcast([P, nh, nk]), ALU.subtract))
                m = mx[:, t, hs]
                step(dve.tensor_reduce(m, o, AX, ALU.max))
                dve.tensor_tensor(nm[:, hs], m, nslope[:, l, hs], ALU.mult).then_inc(score_out, 1)

            def at_turn_of(l, n):
                if l == 0:
                    return 1 + n + 1
                return 1 + 6 + 4 + 20 + (n - 6) + 1

            def combine(n, j):
                t, hs, nh, nk = att_fill(0, j)
                dve.wait_ge(p_ready, n + 1)
                r = rden[:, t, hs]
                step(dve.reciprocal(r, den_ev[:, t, hs]))
                step(dve.tensor_tensor(r, r, lamrow[:, hs], ALU.mult))
                for v in range(nh // 2):
                    p1 = sc[n % 2][:, 2 * v * nk:(2 * v + 1) * nk]
                    p2 = sc[n % 2][:, (2 * v + 1) * nk:(2 * v + 2) * nk]
                    step(dve.tensor_scalar(p2, p2, r[:, 2 * v + 1:2 * v + 2], None, ALU.mult))
                    ins = dve.scalar_tensor_tensor(out=p1, in0=p1, scalar=r[:, 2 * v:2 * v + 1], in1=p2,
                                                   op0=ALU.mult, op1=ALU.add)
                ins.then_inc(a_ready, 1)

            def sub_norm(t):
                misc_in()
                dve.tensor_copy(oo, bank[7][:, :]).then_inc(misc_free, 1)
                dve.wait_ge(misc_free, misc.n)
                o4 = oo.rearrange("p (h n) -> p h n", h=4)
                b4 = vg[:, t, :].rearrange("p (h n) -> p h n", h=4)
                step(dve.tensor_tensor(vg[:, t, :], oo, oo, ALU.mult))
                step(dve.tensor_reduce(ms4[:, 0:4], b4, AX, ALU.add))
                dve.tensor_scalar(ms4[:, 0:4], ms4[:, 0:4], 1.0 / P, RMS_EPS, ALU.mult, ALU.add).then_inc(pow_asked, 1)
                dve.wait_ge(pow_done, 4 + t)
                step(dve.tensor_tensor(o4, o4, ms4[:, 4:8].unsqueeze(2).to_broadcast([P, 4, P]), ALU.mult))
                dve.scalar_tensor_tensor(out=b4, in0=o4, scalar=1.0 - LAM_INIT,
                                         in1=row[:, R_SUBG:R_SUBG + P].unsqueeze(1).to_broadcast([P, 4, P]),
                                         op0=ALU.mult, op1=ALU.mult).then_inc(bout_ready, 1)

            def residual(l, f):
                for k in range(4):
                    j, t = k // 2, k % 2
                    wait_fill(dve, l, f + k)
                    tmp = scr[:, 8192 + 512 * (k % 2):8704 + 512 * (k % 2)]
                    sem_, n = emptied(l, f + k)
                    dve.tensor_tensor(tmp, fill_bank(f + k)[:, :], gb[:, 0, j * W:(j + 1) * W], ALU.mult)\
                       .then_inc(sem_, 1)
                    dve.wait_ge(sem_, n)
                    xx = xs[:, t, j * W:(j + 1) * W]
                    step(dve.tensor_tensor(xx, xx, tmp, ALU.add))

            def even():
                dve.wait_ge(rows_in, 16)
                for k in range(2):
                    o = R_LAM + 128 * k
                    step(dve.tensor_tensor(lam_p[:, k, :], row[:, o:o + 64], row[:, o + 64:o + 128], ALU.mult))
                dve.tensor_reduce(lam_t[:, 0:2], lam_p, AX, ALU.add).then_inc(lam_part, 1)
                for t in range(T):
                    dve.wait_ge(fill_act[0], t + 1)
                    step(dve.bn_stats(stat[:, 6 * t:6 * t + 6], vg[:, t, :]))
                    step(dve.bn_aggr(mv[:, 0:2], stat[:, 6 * t:6 * t + 6]))
                    dve.tensor_scalar(mv[:, 3:4], mv[:, 1:2], LN_EPS, None, ALU.add).then_inc(pow_asked, 1)
                    dve.wait_ge(pow_done, 2 + t)
                    step(dve.tensor_scalar(vn[:, t, :], vg[:, t, :], mv[:, 0:1], mv[:, 2:3], ALU.subtract, ALU.mult))
                    step(dve.tensor_tensor(vn[:, t, :], vn[:, t, :], row[:, R_LNG:R_LNG + 512], ALU.mult))
                    dve.tensor_tensor(vn[:, t, :], vn[:, t, :], row[:, R_LNB:R_LNB + 512], ALU.add).then_inc(vn_ready, 1)
                dve.wait_ge(lam_exp, 1)
                step(dve.tensor_tensor(lam_t[:, 0:1], lam_t[:, 3:4], lam_t[:, 2:3], ALU.subtract))
                step(dve.memset(lamrow, 1.0))
                lr = lamrow.rearrange("p (h m) -> p h m", m=2)[:, :, 1]
                step(dve.tensor_scalar(lr, lam_t[:, 0:1].to_broadcast([P, 4]), -LAM_INIT, None, ALU.add))
                ada(4)
                ada(5)
                ada_out(0, 4)
                ada(6)
                ada_out(0, 5)
                for h in range(2):
                    wait_fill(dve, 0, 4 + h)
                    dve.tensor_copy(kT[0][:, 2 * h:2 * h + 2, :], fill_bank(4 + h)[:, :].rearrange("p (c n) -> p c n", c=2))\
                       .then_inc(fill_dve[0], 1)
                ada_out(0, 6)
                dve.wait_ge(dist_done, 2)
                scores(0, 0, 0, sc, nm_ev[:, 0, :], 0)
                scores(0, 1, 1, sc, nm_ev[:, 0, :], 0)
                ada(7)
                combine(0, 0)
                ada(8)
                for h in range(2):
                    wait_fill(dve, 0, 6 + h)
                    dve.tensor_copy(vv[:, h, :], fill_bank(6 + h)[:, :]).then_inc(fill_dve[0], 1)
                ada_out(0, 7)
                ada_out(0, 8)
                for j in range(2, 6):
                    scores(0, j, j, sc, nm_ev[:, 1, :], 0)
                    combine(j - 1, j - 1)
                    if j == 3:
                        sub_norm(0)
                        ada(9)
                        ada_out(0, 9)
                    if j == 4:
                        ada(10)
                combine(5, 5)
                ada(11)
                sub_norm(1)
                ada_out(0, 10)
                ada_out(0, 11)
                gates_out()
                for t in range(T):
                    dve.wait_ge(sgu_mixed, t + 1)
                    dve.wait_ge(fill_act[0], 5 + t)
                    for g in range(4):
                        o = uu[:, t, g * P:(g + 1) * P]
                        ins = dve.scalar_tensor_tensor(out=o, in0=bank[4 + t][:, g * P:(g + 1) * P],
                                                       scalar=col[:, C_SGUB + g:C_SGUB + g + 1], in1=o,
                                                       op0=ALU.add, op1=ALU.mult)
                    ins.then_inc(aout_ready, 1)
                residual(0, 10)

            def odd():
                step(dve.memset(glu[:, :, 0:TAPS - 1], 0.0))
                for h in range(2):
                    wait_fill(dve, 1, 2 + h)
                    dve.wait_ge(fill_act[1], h + 1)
                    dve.tensor_tensor(glu[:, 2 * h:2 * h + 2, TAPS - 1:TAPS - 1 + 256],
                                      fill_bank(2 + h)[:, :].rearrange("p (c n) -> p c n", c=2),
                                      sg[:, 2 * h:2 * h + 2, :], ALU.mult).then_inc(fill_dve[1], 1)
                dve.wait_ge(fill_dve[1], 2)
                n_conv = [0]

                def taps(js):
                    for j in js:
                        for c in range(4):
                            src = glu[:, c, j:j + 256]
                            w = col[:, C_CONVW + c * TAPS + j:C_CONVW + c * TAPS + j + 1]
                            if j == 0:
                                ins = dve.tensor_scalar(conv[:, c, :], src, w, col[:, C_CONVB + c:C_CONVB + c + 1],
                                                        ALU.mult, ALU.add)
                            else:
                                dve.wait_ge(conv_step, n_conv[0] - 3)
                                ins = dve.scalar_tensor_tensor(out=conv[:, c, :], in0=src, scalar=w, in1=conv[:, c, :],
                                                               op0=ALU.mult, op1=ALU.add)
                            n_conv[0] += 1
                            if n_conv[0] < 4 * TAPS:
                                ins.then_inc(conv_step, 1)
                            else:
                                ins.then_inc(conv_ready, 1)

                def group(g, between):
                    for j in range(6):
                        t = att_fill(1, j)[0]
                        scores(1, 6 + 6 * g + j, j, sc_o, nm_od[:, g, 8 * t:8 * t + 8], 1 + g)
                        if j == 1:
                            between[0]()
                        if j == 5:
                            between[2]()
                        if j in (3, 5):
                            tt = 0 if j == 3 else 1
                            misc_in()
                            dve.tensor_copy(og[:, g, 8 * tt:8 * tt + 8, :],
                                            bank[7][:, :].rearrange("p (h n) -> p h n", h=8)).then_inc(misc_free, 1)
                        if j == 3:
                            between[1]()
                    between[3]()

                def ada_odd(j):
                    ada_acc(acc_mixer, j, pre_place(1, ("ada", j)))

                ada_n[0] = 20
                nothing = lambda: None
                taps(range(22))
                group(0, [lambda: taps(range(22, 25)), lambda: taps(range(25, 28)), lambda: taps(range(28, 31)),
                          lambda: ada_odd(8)])
                misc_in()
                dve.scalar_tensor_tensor(out=conv, in0=bank[7][:, 0:256].unsqueeze(1).to_broadcast([P, 4, 256]),
                                         scalar=-1.0 / 512, in1=conv, op0=ALU.mult, op1=ALU.add).then_inc(misc_free, 1)
                dve.wait_ge(misc_free, misc.n)
                dve.tensor_copy(stat[:, 0:1], conv[:, 0, 0:1]).then_inc(xc_ready, 1)
                ada_out(1, 8)

                def conv_rms():
                    misc_in()
                    dve.tensor_scalar(mv[:, 0:2], bank[7][:, 0:2], 1.0 / 512, LN_EPS, ALU.mult, ALU.add)\
                       .then_inc(misc_free, 1)
                    dve.wait_ge(misc_free, misc.n)
                    dve.tensor_copy(stat[:, 1:2], mv[:, 0:1]).then_inc(pow_asked, 1)
                    dve.wait_ge(pow_done, 8)
                    for t in range(T):
                        ins = dve.tensor_scalar(sg[:, 0, t * P:(t + 1) * P], ident[:, :], mv[:, 2 + t:3 + t], None, ALU.mult)
                    ins.then_inc(diag_ready, 1)

                def conv_norm():
                    misc_in()
                    dve.tensor_tensor(conv, bank[7][:, 0:256].unsqueeze(1).to_broadcast([P, 4, 256]), conv, ALU.mult)\
                       .then_inc(misc_free, 1)
                    dve.wait_ge(misc_free, misc.n)
                    dve.tensor_copy(stat[:, 2:3], conv[:, 0, 0:1]).then_inc(xn_ready, 1)
                    ada_odd(9)
                    ada_out(1, 9)

                group(1, [conv_rms, conv_norm, lambda: ada_odd(10), lambda: ada_odd(11)])
                ada_out(1, 10)
                ada_out(1, 11)
                group(2, [nothing] * 4)
                step(dve.tensor_tensor(nmin, nm_od[:, 0, :], nm_od[:, 1, :], ALU.min))
                step(dve.tensor_tensor(nmin, nmin, nm_od[:, 2, :], ALU.min))
                dve.tensor_tensor(e_od, nmin.unsqueeze(1).to_broadcast([P, 3, 16]), nm_od, ALU.subtract)\
                   .then_inc(ediff_ready, 1)
                dve.wait_ge(e_ready, 1)
                step(dve.tensor_tensor(w_od, e_od, den_od, ALU.mult))
                step(dve.tensor_tensor(wsum, w_od[:, 0, :], w_od[:, 1, :], ALU.add))
                step(dve.tensor_tensor(wsum, wsum, w_od[:, 2, :], ALU.add))
                step(dve.reciprocal(wsum, wsum))
                step(dve.tensor_tensor(w_od, e_od, wsum.unsqueeze(1).to_broadcast([P, 3, 16]), ALU.mult))
                dve.wait_ge(misc_free, misc.n)
                for g in range(3):
                    step(dve.tensor_tensor(og[:, g], og[:, g], w_od[:, g, :].unsqueeze(2).to_broadcast([P, 16, 64]), ALU.mult))
                cc = qT[0].rearrange("p a b -> p (a b)").rearrange("p (h n) -> p h n", h=16)
                step(dve.tensor_tensor(cc, og[:, 0], og[:, 1], ALU.add))
                dve.tensor_tensor(cc, cc, og[:, 2], ALU.add).then_inc(cout_ready, 1)
                gates_out()
                residual(1, 18)

            def first_of(dst, vals, width, one, tmp):
                step(dve.tensor_reduce(one, vals, AX, ALU.max))
                bc = one.unsqueeze(2).to_broadcast([P, 2, width])
                no = no16[:, 0:width].unsqueeze(1).to_broadcast([P, 2, width])
                step(dve.tensor_tensor(tmp, vals, bc, ALU.is_lt))
                step(dve.scalar_tensor_tensor(out=tmp, in0=tmp, scalar=64.0, in1=no, op0=ALU.mult, op1=ALU.add))
                step(dve.tensor_reduce(one, tmp, AX, ALU.min))
                step(dve.tensor_tensor(dst, no, bc, ALU.is_equal))

            def route(l):
                misc_in()
                logits = bank[7][:, 0:32].rearrange("p (t e) -> p t e", t=2)
                step(dve.tensor_reduce(one2[0], logits, AX, ALU.max))
                dve.tensor_tensor(lg, logits, one2[0].unsqueeze(2).to_broadcast([P, 2, 16]), ALU.subtract)\
                   .then_inc(misc_free, 1)
                dve.wait_ge(misc_free, misc.n)
                dve.tensor_copy(one2[5][:, 0:1], lg[:, 0, 0:1]).then_inc(lgm_ready, 1)
                dve.wait_ge(pr_ready, l + 1)
                step(dve.tensor_reduce(one2[0], pr, AX, ALU.add))
                step(dve.reciprocal(one2[0], one2[0]))
                step(dve.tensor_tensor(pr, pr, one2[0].unsqueeze(2).to_broadcast([P, 2, 16]), ALU.mult))
                step(dve.tensor_tensor(sel, pr, rb_row[:, :].unsqueeze(1).to_broadcast([P, 2, 16]), ALU.add))
                q = sel.rearrange("p t (g k) -> p t g k", k=4)
                hi1, lo1, hi2, lo2, sc4, tmp4 = g4
                dve.tensor_tensor(hi1, q[:, :, :, 0], q[:, :, :, 1], ALU.max)
                dve.tensor_tensor(lo1, q[:, :, :, 0], q[:, :, :, 1], ALU.min)
                dve.tensor_tensor(hi2, q[:, :, :, 2], q[:, :, :, 3], ALU.max)
                step(dve.tensor_tensor(lo2, q[:, :, :, 2], q[:, :, :, 3], ALU.min))
                step(dve.tensor_tensor(sc4, hi1, hi2, ALU.max))
                step(dve.tensor_tensor(hi1, hi1, hi2, ALU.min))
                step(dve.tensor_tensor(lo1, lo1, lo2, ALU.max))
                step(dve.tensor_tensor(hi1, hi1, lo1, ALU.max))
                step(dve.tensor_tensor(sc4, sc4, hi1, ALU.add))
                first_of(oh, sc4, 4, one2[1], tmp4)
                dve.tensor_copy(one2[5][:, 1:2], oh[:, 0, 0:1]).then_inc(oh_ready, 1)
                for t in range(T):
                    step(dve.tensor_tensor(s16[:, t, :].rearrange("p (g k) -> p g k", k=4), q[:, t],
                                           oh[:, t, :].unsqueeze(2).to_broadcast([P, 4, 4]), ALU.mult))
                    step(dve.tensor_scalar(oh1[:, t, :].rearrange("p (g k) -> p g k", k=4),
                                           oh[:, t, :].unsqueeze(2).to_broadcast([P, 4, 4]), 1e30, -1e30, ALU.mult, ALU.add))
                step(dve.tensor_tensor(s16, s16, oh1, ALU.add))
                first_of(oh1, s16, 16, one2[2], oh2)
                step(dve.scalar_tensor_tensor(out=s16, in0=oh1, scalar=-1e32, in1=s16, op0=ALU.mult, op1=ALU.add))
                first_of(oh2, s16, 16, one2[2], gates)
                step(dve.tensor_tensor(oh1, oh1, oh2, ALU.add))
                step(dve.tensor_tensor(gates, pr, oh1, ALU.mult))
                step(dve.tensor_reduce(one2[3], gates, AX, ALU.add))
                step(dve.reciprocal(one2[3], one2[3]))
                step(dve.tensor_tensor(gates, gates, one2[3].unsqueeze(2).to_broadcast([P, 2, 16]), ALU.mult))
                misc_in()
                step(dve.tensor_copy(rank.rearrange("p t g -> p (t g)"), bank[7][:, 0:8]))
                dve.tensor_copy(cnt, bank[7][:, 8:12]).then_inc(misc_free, 1)
                dve.wait_ge(misc_free, misc.n)
                step(dve.tensor_scalar(rank2, rank, -float(CAP), None, ALU.add))
                step(dve.tensor_reduce(cmax, cnt, AX, ALU.max))
                dve.tensor_scalar(flag[:, l:l + 1], cmax, float(CAP), None, ALU.is_gt).then_inc(flag_ready, 1)

            def slot_map(dst, g, numbers, ranks):
                for t in range(T):
                    ins = dve.tensor_scalar(dst[:, t, :], numbers[:, :], ranks[:, t, bass.ds(g, 1)], oh[:, t, bass.ds(g, 1)],
                                            ALU.is_equal, ALU.mult)
                return ins

            def gather_cols(gg, l, half, src):
                for c in range(4):
                    cc = 4 * half + c
                    ins = dve.tensor_scalar(hg[gg][:, cc, :], src[:, c * P:(c + 1) * P], scale(l, 1, cc),
                                            shift(l, 1, cc), ALU.mult, ALU.add)
                return ins

            def y_out_gated(l, s_, n):
                for h in range(2):
                    ins = dve.tensor_tensor(ysb[:, h * W:(h + 1) * W], bank[4 + h][:, :],
                                            gb[:, 1, h * W:(h + 1) * W], ALU.mult)
                ins.then_inc(s_, n)

            def add_x(k, b):
                t, h = k // 2, k % 2
                xx = xs[:, t, h * W:(h + 1) * W]
                return dve.tensor_tensor(xx, b[:, :], xx, ALU.add)

            def experts(l):
                with dve.Fori(0, 2) as i:
                    misc.enter(l, i)
                    n0 = 16 * l
                    ada_n[0] = 12

                    def slot_gates(gg):
                        misc_in()
                        dve.tensor_copy(gslot[:, gg, :], bank[7][:, 0:4]).then_inc(misc_free, 1)

                    def gather(gg):
                        misc_in()
                        gather_cols(gg, l, 1, bank[7]).then_inc(misc_free, 1)
                        dve.wait_ge(misc_free, misc.value())
                        dve.tensor_copy(h_hi[:, gg, 4:8, :], hg[gg][:, 4:8, :]).then_inc(h_hi_dve, 1)
                        dve.wait_ge(h_hi_dve, i * 2 + (4 * l + gg + 1))
                        dve.tensor_tensor(h_lo[:, gg, 4:8, :], hg[gg][:, 4:8, :], h_hi[:, gg, 4:8, :].bitcast(F32),
                                          ALU.subtract).then_inc(h_ready, 1)
                        dve.wait_ge(h_hi_act, i * 2 + (4 * l + gg + 1))
                        dve.tensor_tensor(h_lo[:, gg, 0:4, :], hg[gg][:, 0:4, :], h_hi[:, gg, 0:4, :].bitcast(F32),
                                          ALU.subtract).then_inc(h_ready, 1)

                    def split(n, kind, quarters=range(4)):
                        pl = body_place(l, (kind, n), i)
                        for q in quarters:
                            k = quarter(n, kind, q)
                            dve.wait_ge(hi_ready, hi_at(l, i, k))
                            ins = dve.tensor_tensor(w_lo[:, k % PARTS, :], raw_quarter(pl, q),
                                                    w_hi[:, k % PARTS, :].bitcast(F32), ALU.subtract)
                            ins.then_inc(*((lo_ready, 1) if q < 3 else (panel_done[pl.slot], 1)))

                    def slot_T(gg):
                        misc_in()
                        dve.tensor_copy(pt[gg].rearrange("p t n -> p (t n)"), bank[7][:, 0:256]).then_inc(misc_free, 1)

                    def misc_x(k):
                        misc_in()
                        add_x(k, bank[7]).then_inc(misc_free, 1)

                    def y_group(gg):
                        pl = body_place(l, ("D", 4 * gg + 3), i)
                        dve.wait_ge(panel_done[pl.slot], pl.done)
                        y_out_gated(l, y_out, 1)

                    slot_map(pcur[0], i * 2, slot_no, rank).then_inc(p_built, 1)
                    split(0, "G", range(2))
                    slot_gates(0)
                    gather(0)
                    split(0, "G", range(2, 4))
                    for n in range(8):
                        split(n, "U")
                        if n == 0:
                            slot_T(0)
                        if n == 2:
                            slot_gates(1)
                        if n in (5, 6):
                            misc_x(0 if n == 5 else 3)
                        if n < 7:
                            split(n + 1, "G", range(3))
                        dve.wait_ge(sil_ready, i * 8 + (n0 + n + 1))
                        dve.wait_ge(part_used, used_at(l, i, quarter(n, "U", 3)))
                        if n in (0, 4):
                            dve.wait_ge(misc_free, misc.value())
                        dve.scalar_tensor_tensor(out=act_t[n % 2], in0=bank[2 * (n % 2) + 1][:, :],
                                                 scalar=gslot[:, n // 4, n % 4:n % 4 + 1], in1=sil[n % 2],
                                                 op0=ALU.mult, op1=ALU.mult).then_inc(act_ready, 1)
                        if n < 7:
                            split(n + 1, "G", range(3, 4))
                        if n == 1:
                            slot_map(pcur[1], i * 2 + 1, slot_no, rank).then_inc(p_built, 1)
                        if n == 2:
                            gather(1)
                        if n == 3:
                            slot_T(1)
                        if n == 5:
                            misc_x(1)
                        if l == 0 and n in ADA_STEPS:
                            a = ADA_STEPS.index(n)
                            ada_acc(acc_experts, a, body_place(0, ("A", a), i), i)
                        if n == 4:
                            y_group(0)
                        if l == 0 and n - 1 in ADA_STEPS:
                            ada_out(1, i * 4 + ADA_STEPS.index(n - 1))
                        if n == 5:
                            misc_x(2)
                    y_group(1)
                    for k in range(4):
                        dve.wait_ge(tail_full, i * 4 + (8 * l + k + 1))
                        add_x(k, bank[k]).then_inc(tail_free, 1)
                    misc.leave()

            def overflow(l):
                dve.wait_ge(flag_ready, l + 1)
                over = dve.value_load(flag[0:1, l:l + 1])
                with dve.If(over > 0):
                    dve.wait_ge(tail_free, 8 * (l + 1))
                    with dve.Fori(0, 4) as g:
                        q, a = g * 15, g * 4
                        slot_map(pcur[0], g, slot_all, rank2).then_inc(ov_dve[l], 1)
                        dve.wait_ge(ov_pe[l], q + 1)
                        dve.tensor_copy(pt[0].rearrange("p t n -> p (t n)"), bank[7][:, 0:256])
                        dve.tensor_copy(gslot[:, 0, :], bank[7][:, 256:260]).then_inc(ov_dve[l], 1)
                        dve.wait_ge(ov_pe[l], q + 2)
                        gather_cols(0, l, 0, bank[6])
                        gather_cols(0, l, 1, bank[7]).then_inc(ov_dve[l], 1)
                        for e in range(4):
                            dve.wait_ge(ov_act[l], a + (e + 1))
                            dve.wait_ge(ov_pe[l], q + (3 + 3 * e))
                            dve.scalar_tensor_tensor(out=act_t[0], in0=bank[1][:, :], scalar=gslot[:, 0, e:e + 1],
                                                     in1=sil[0], op0=ALU.mult, op1=ALU.mult).then_inc(ov_dve[l], 1)
                            dve.wait_ge(ov_pe[l], q + (4 + 3 * e))
                            dve.tensor_copy(actT[0].rearrange("p c n -> p (c n)"), bank[6][:, :]).then_inc(ov_dve[l], 1)
                        dve.wait_ge(ov_pe[l], q + 14)
                        y_out_gated(l, ov_dve[l], 1)
                        dve.wait_ge(ov_pe[l], q + 15)
                        for k in range(4):
                            ins = add_x(k, bank[k])
                        ins.then_inc(ov_dve[l], 1)
                    dve.wait_ge(ov_dve[l], 52)

            dve.wait_ge(cact_ready, 1)
            ada(0)
            for j in range(1, 4):
                ada(j)
                ada_out(0, j - 1)
            ada_out(0, 3)
            open_phase(0)
            norm(0)
            dve.wait_ge(turn_full, 1)
            dve.memset(qz[0][64:128, :, :], 0.0)
            dve.memset(qz[1][0:64, :, :], 0.0).then_inc(qz_zero, 1)
            dve.wait_ge(dist_i, 2)
            distances()
            even()
            open_phase(1)
            norm(1)
            dve.wait_ge(rb_in, 16)
            route(0)
            experts(0)
            dve.wait_ge(tail_free, 8)
            overflow(0)
            open_phase(2)
            norm(2)
            odd()
            open_phase(3)
            norm(3)
            route(1)
            experts(1)
            dve.wait_ge(tail_free, 16)
            overflow(1)
            dve.memset(stat[:, 0:1], 0.0).then_inc(x_ready, 1)
            rstd_of(4)
            dve.wait_ge(pow_done, NORM_ROOT[4])
            dve.wait_ge(fg_in, 16)
            for t in range(T):
                dve.scalar_tensor_tensor(out=xh[:, t, :], in0=xs[:, t, :], scalar=rstd[:, t:t + 1], in1=fgrow,
                                         op0=ALU.mult, op1=ALU.mult).then_inc(final_ready, 1)


def kernel(x, c, norm1_g, norm2_g, ada_w, ada_b, ev_w_in, ev_w_out, sgu_ln_g, sgu_ln_b, sgu_w, sgu_b, lam_q1, lam_k1,
           lam_q2, lam_k2, diff_subln_g, od_w_in, od_w_out, conv_w, conv_b, conv_ln_g, conv_ln_b, router_w, router_b,
           moe_w_gu, moe_w_down, final_g):
    import numpy as np
    import concourse.bacc as bacc
    from concourse.bass_utils import run_bass_kernel_spmd

    def by_partition(a):
        a = np.asarray(a)
        a = a.reshape(-1, a.shape[-1] // P, P)
        return a.transpose(2, 0, 1).reshape(P, -1)

    n1, n2 = np.asarray(norm1_g), np.asarray(norm2_g)
    cols = np.concatenate([
        by_partition(c), by_partition(np.stack([n1[0], n2[0], n1[1], n2[1]])), by_partition(ada_b),
        by_partition(conv_b), by_partition(conv_ln_g), by_partition(conv_ln_b),
        np.asarray(conv_w)[0].reshape(TAPS, 4, P).transpose(2, 1, 0).reshape(P, -1),
        np.asarray(sgu_b)[0].T,
        np.asarray(router_w).reshape(KC, P, 16).transpose(1, 0, 2).reshape(P, -1)], axis=1)
    rows = np.concatenate([np.asarray(a).reshape(-1) for a in (
        sgu_ln_g, sgu_ln_b, diff_subln_g, lam_q1, lam_k1, lam_q2, lam_k2)])
    arrays = {"x": np.asarray(x)[0], "cols": cols, "rows": rows, "router_b": router_b, "ada_w": ada_w,
              "ev_w_in": ev_w_in, "ev_w_out": ev_w_out, "sgu_w": sgu_w, "od_w_in": od_w_in, "od_w_out": od_w_out,
              "w_gu": moe_w_gu, "w_down": moe_w_down, "final_g": final_g}
    arrays = {f"{n}_dram": np.ascontiguousarray(a) for n, a in arrays.items()}
    nc = bacc.Bacc("TRN2", target_bir_lowering=False, num_devices=1)
    args = [nc.dram_tensor(n, a.shape, mybir.dt.from_np(a.dtype), kind="ExternalInput").ap() for n, a in arrays.items()]
    y = nc.dram_tensor("y_dram", (T * P, D), F32, kind="ExternalOutput").ap()
    trunk(nc, *args, y)
    r = run_bass_kernel_spmd(nc, [arrays], core_ids=[0])
    return r.results[0]["y_dram"].reshape(1, T * P, D)
```
